# Optimizing a Trainium2 kernel written in Bass

```python
import jax, jax.numpy as jnp
from jax import lax
import numpy as np

D_MODEL = 1024
BATCH = 1
SEQ = 512
DEPTH = 1

EPS = 1e-6
SGU_CHUNK = 128
SGU_GROUPS = 8
SGU_WIDTH = D_MODEL
SGU_GROUP_DIM = SGU_WIDTH // SGU_GROUPS
GLA_HEADS = 4
GLA_DK = D_MODEL // 2
GLA_DV = D_MODEL
GLA_HEAD_DK = GLA_DK // GLA_HEADS
GLA_HEAD_DV = GLA_DV // GLA_HEADS
GLA_LOWRANK = 16
GLA_GATE_NORMALIZER = 16.0
GLA_CHUNK = 64
D_FF = -(-(8 * D_MODEL) // (3 * 256)) * 256
IN_SIZES = (SGU_WIDTH, SGU_WIDTH, GLA_DK, GLA_DK, GLA_DV, GLA_DV, GLA_LOWRANK, D_MODEL, D_MODEL)
IN_COLS = 2 * SGU_WIDTH + 2 * GLA_DK + 2 * GLA_DV + GLA_LOWRANK + 2 * D_MODEL

kernel_name = "hybrid_gmlp_gla_gated_merge"

def rms_norm(x, w):
    xf = x.astype(jnp.float32)
    y = xf * lax.rsqrt(jnp.mean(xf * xf, axis=-1, keepdims=True) + EPS)
    return (y * w.astype(jnp.float32)).astype(x.dtype)

def layer_norm(x, w, b):
    xf = x.astype(jnp.float32)
    mu = jnp.mean(xf, axis=-1, keepdims=True)
    var = jnp.mean(jnp.square(xf - mu), axis=-1, keepdims=True)
    y = (xf - mu) * lax.rsqrt(var + EPS)
    return (y * w.astype(jnp.float32) + b.astype(jnp.float32)).astype(x.dtype)

def chunked_sgu(u, v, ln_w, ln_b, w_s, b_s):
    B, S, _ = v.shape
    n = S // SGU_CHUNK
    v = layer_norm(v, ln_w, ln_b)
    vc = v.reshape(B, n, SGU_CHUNK, SGU_GROUPS, SGU_GROUP_DIM)
    mask = jnp.tril(jnp.ones((SGU_CHUNK, SGU_CHUNK), dtype=bool))
    w = jnp.where(mask[None], w_s, jnp.zeros_like(w_s)).astype(v.dtype)
    mixed = jnp.einsum('gts,bnsgc->bntgc', w, vc) + b_s.T.astype(v.dtype)[:, :, None]
    return u * mixed.reshape(B, S, SGU_WIDTH)

def gla(q, k, v, gk, r, norm_w):
    out_dtype = q.dtype
    B, S, _ = q.shape
    n = S // GLA_CHUNK

    def heads(t, d):
        return t.astype(jnp.float32).reshape(B, n, GLA_CHUNK, GLA_HEADS, d).transpose(0, 3, 1, 2, 4)

    qh = heads(q, GLA_HEAD_DK) * (GLA_HEAD_DK ** -0.5)
    kh = heads(k, GLA_HEAD_DK)
    vh = heads(v, GLA_HEAD_DV)
    g = heads(gk, GLA_HEAD_DK)
    b = jnp.cumsum(g, axis=3)
    b_last = b[:, :, :, -1:, :]
    q_dec = qh * jnp.exp(b)
    k_dec = kh * jnp.exp(-b)
    k_end = kh * jnp.exp(b_last - b)
    mask = jnp.tril(jnp.ones((GLA_CHUNK, GLA_CHUNK), dtype=bool))
    scores = jnp.einsum('bhntd,bhnsd->bhnts', q_dec, k_dec)
    scores = jnp.where(mask, scores, 0.0)
    o_intra = jnp.einsum('bhnts,bhnsv->bhntv', scores, vh)
    kv = jnp.einsum('bhnsd,bhnsv->bhndv', k_end, vh)
    decay = jnp.exp(b_last[:, :, :, 0, :])

    def step(state, inp):
        dec, kv_n = inp
        return dec[..., None] * state + kv_n, state

    s0 = jnp.zeros((B, GLA_HEADS, GLA_HEAD_DK, GLA_HEAD_DV), jnp.float32)
    _, s_prev = lax.scan(step, s0, (jnp.moveaxis(decay, 2, 0), jnp.moveaxis(kv, 2, 0)))
    s_prev = jnp.moveaxis(s_prev, 0, 2)
    o = o_intra + jnp.einsum('bhntd,bhndv->bhntv', q_dec, s_prev)
    o = o * lax.rsqrt(jnp.mean(o * o, axis=-1, keepdims=True) + EPS) * norm_w.astype(jnp.float32)
    o = o.transpose(0, 2, 3, 1, 4).reshape(B, S, GLA_DV)
    return (o * jax.nn.silu(r.astype(jnp.float32))).astype(out_dtype)

def setup_inputs(seed: int = 0) -> dict:
    key = jax.random.key(seed)
    ks = jax.random.split(key, 24)
    L = DEPTH
    nrm = jax.random.normal

    def dense(k, fan_in, fan_out):
        return nrm(k, (L, fan_in, fan_out), jnp.float32) * fan_in ** -0.5

    def gain(k, d):
        return 1.0 + 0.05 * nrm(k, (L, d), jnp.float32)

    return {
        "x": nrm(ks[0], (BATCH, SEQ, D_MODEL), jnp.float32),
        "norm1_w": gain(ks[1], D_MODEL),
        "w_in": dense(ks[2], D_MODEL, IN_COLS),
        "b_in": 0.02 * nrm(ks[3], (L, IN_COLS), jnp.float32),
        "sgu_ln_w": gain(ks[4], SGU_WIDTH),
        "sgu_ln_b": 0.02 * nrm(ks[5], (L, SGU_WIDTH), jnp.float32),
        "sgu_w": 0.5 * SGU_CHUNK ** -0.5 * nrm(ks[6], (L, SGU_GROUPS, SGU_CHUNK, SGU_CHUNK), jnp.float32),
        "sgu_b": 1.0 + 0.1 * nrm(ks[7], (L, SGU_GROUPS, SGU_CHUNK), jnp.float32),
        "w_gk2": dense(ks[8], GLA_LOWRANK, GLA_DK),
        "b_gk": 0.1 * nrm(ks[9], (L, GLA_DK), jnp.float32),
        "gla_norm_w": gain(ks[10], GLA_HEAD_DV),
        "w_branch_a": dense(ks[11], SGU_WIDTH, D_MODEL),
        "w_branch_b": dense(ks[12], GLA_DV, D_MODEL),
        "w_out": dense(ks[13], D_MODEL, D_MODEL),
        "norm2_w": gain(ks[14], D_MODEL),
        "w_ffn_gate": dense(ks[15], D_MODEL, D_FF),
        "w_ffn_up": dense(ks[16], D_MODEL, D_FF),
        "w_ffn_down": dense(ks[17], D_FF, D_MODEL),
        "final_norm_w": 1.0 + 0.05 * nrm(ks[18], (D_MODEL,), jnp.float32),
    }

def reference(x, norm1_w, w_in, b_in, sgu_ln_w, sgu_ln_b, sgu_w, sgu_b, w_gk2, b_gk,
              gla_norm_w, w_branch_a, w_branch_b, w_out, norm2_w, w_ffn_gate, w_ffn_up,
              w_ffn_down, final_norm_w):
    split_points = [int(s) for s in np.cumsum(IN_SIZES)[:-1]]
    h = x
    for l in range(DEPTH):
        xn = rms_norm(h, norm1_w[l])
        proj = xn @ w_in[l] + b_in[l]
        u, v, q, k, vg, r, g_lr, gate_a, gate_b = jnp.split(proj, split_points, axis=-1)
        ya = chunked_sgu(jax.nn.gelu(u), jax.nn.gelu(v), sgu_ln_w[l], sgu_ln_b[l], sgu_w[l], sgu_b[l])
        gk = jax.nn.log_sigmoid((g_lr @ w_gk2[l] + b_gk[l]).astype(jnp.float32)) / GLA_GATE_NORMALIZER
        yb = gla(q, k, vg, gk, r, gla_norm_w[l])
        merged = jax.nn.sigmoid(gate_a) * (ya @ w_branch_a[l]) + jax.nn.sigmoid(gate_b) * (yb @ w_branch_b[l])
        h = h + merged @ w_out[l]
        xn2 = rms_norm(h, norm2_w[l])
        h = h + (jax.nn.silu(xn2 @ w_ffn_gate[l]) * (xn2 @ w_ffn_up[l])) @ w_ffn_down[l]
    return rms_norm(h, final_norm_w)


_drawn_inputs = setup_inputs


def setup_inputs(seed=0):
    import zlib

    import numpy as np

    out = dict(_drawn_inputs(seed))
    spreads = {}
    factors = {'b_in': 3.514,
     'sgu_ln_w': 8.0,
     'sgu_ln_b': 38.011,
     'b_gk': 4.032,
     'gla_norm_w': 3.379,
     'sgu_b': 2.785,
     'norm2_w': 2.834}
    for name, (base, spread) in spreads.items():
        noise = np.random.default_rng([zlib.crc32(name.encode()), seed]).standard_normal(out[name].shape)
        drawn = base * np.exp(spread * noise) if base else spread * noise
        out[name] = __import__('jax').numpy.asarray(drawn.astype(out[name].dtype))
    for name, factor in factors.items():
        out[name] = (out[name] * factor).astype(out[name].dtype)
    return out
```

```python
from contextlib import ExitStack

import numpy as np

import concourse.bass as bass
from concourse import mybir

ALU = mybir.AluOpType
ACT = mybir.ActivationFunctionType
F32 = mybir.dt.float32
F32R = mybir.dt.float32r
BF16 = mybir.dt.bfloat16
U8 = mybir.dt.uint8

P = 128
SEQ = 512
D = 1024
TT = SEQ // P
KD = D // P
HEADS = 4
DK = 128
DV = 256
CHUNK = 64
NCH = SEQ // CHUNK
GROUPS = 8
LOWRANK = 16
DFF = 2816
KF = DFF // P
EPS = 1e-6
GATE_NORM = 16.0
KV_BANKS = (2, 3, 6, 7)
BLK = 2048
HALF = 512

C_U, C_V, C_Q, C_K, C_VG, C_R, C_LR, C_GA, C_GB = 0, 1024, 2048, 2560, 3072, 4096, 5120, 5136, 6160

B_VG = 0
B_QK = 8
B_RU = 12
B_MERGE = 20
B_OUT = 36
B_FFN = 40
FFN_IT = DFF // 256
B_DOWN = B_FFN + 2 * FFN_IT
DOWN_BLKS = KF // 2
N_BLKS = B_DOWN + DOWN_BLKS

K_QK, K_LR, K_R, K_U, K_GA, K_GB, K_BGK, K_GN, K_N1, K_N2, K_END = 0, 8, 9, 17, 25, 33, 41, 45, 47, 55, 63

KB = 1024
BASE = 16512


def build(nc, x, wstream, w_lr, cols, vbias, lnw, lnb, sgub, sgu_wt, w_gk2, ident_d, causal_d, finalw, out):
    with ExitStack() as ctx:
        def sb(name, kb, shape, dtype=F32):
            return nc.alloc_sbuf_tensor_at(name, shape, dtype, offset=BASE + int(kb * KB))

        def sem(name):
            return ctx.enter_context(nc.semaphore(name))

        raw = [sb(f"raw{s}", 8 * s, [P, BLK]) for s in range(2)]
        w_hi = [sb(f"w_hi{s}", 16 + 8 * s, [P, BLK], F32R) for s in range(2)]
        w_lo = [sb(f"w_lo{s}", 32 + 8 * s, [P, BLK], F32R) for s in range(2)]
        xt_hi = sb("xt_hi", 48, [P, KD, SEQ], F32R)
        xt_lo = sb("xt_lo", 64, [P, KD, SEQ], F32R)
        vgs = sb("vgs", 80, [P, 2, TT, D])
        ya_hi = sb("ya_hi", 80, [P, KD, SEQ], F32R)
        ya_lo = sb("ya_lo", 96, [P, KD, SEQ], F32R)
        h = sb("h", 80, [P, TT, D])
        hn = sb("hn", 96, [P, 2, D])
        htmp = sb("htmp", 104, [P, 2, 4, P])
        fw = sb("fw", 108, [P, D])
        xn_in = sb("xn_in", 112, [P, TT, D])
        vbias_bc = sb("vbias_bc", 128, [P, 2, D])
        lnw_bc = sb("lnw_bc", 136, [P, D])
        lnb_bc = sb("lnb_bc", 140, [P, D])
        ya = sb("ya", 112, [P, KD, SEQ])
        yb = sb("yb", 128, [P, KD, SEQ])
        mg_hi = sb("mg_hi", 112, [P, KD, SEQ], F32R)
        mg_lo = sb("mg_lo", 128, [P, KD, SEQ], F32R)
        act = sb("act", 112, [P, KF, SEQ])
        qk = sb("qk", 144, [P, 2 * HEADS, SEQ])
        yb_hi = sb("yb_hi", 144, [P, KD, SEQ], F32R)
        yb_lo = sb("yb_lo", 160, [P, KD, SEQ], F32R)
        xnat = sb("xnat", 160, [P, 2, D])
        xtmp = sb("xtmp", 168, [P, 2, 4, P])
        sq_junk0 = sb("sq_junk0", 172, [P, D])
        sq_junk = sb("sq_junk", 160, [P, D])
        sq_junk2 = sb("sq_junk2", 176, [P, D])
        g = sb("g", 160, [P, HEADS, SEQ])
        cum = sb("cum", 168, [P, NCH, CHUNK])
        rest = sb("rest", 170, [P, NCH, CHUNK])
        expb = sb("expb", 172, [P, NCH, CHUNK])
        ah = [sb(f"ah{s}", 160 + 4 * s, [P, 2, SEQ], F32R) for s in range(2)]
        al = [sb(f"al{s}", 168 + 4 * s, [P, 2, SEQ], F32R) for s in range(2)]
        ken = sb("ken", 176, [P, TT, P])
        osq = sb("osq", 176, [P, SEQ])
        sct = sb("sct", 178, [P, TT, P])
        vst = sb("vst", 180, [P, TT, DV])
        vns = sb("vns", 184, [P, TT, DV])
        state = sb("state", 188, [P, NCH - 1, DV])
        rs = sb("rs", 195, [P, SEQ])
        lr_raw = sb("lr_raw", 180, [P, KD, P])
        lr_hi = sb("lr_hi", 184, [P, KD, P], F32R)
        lr_lo = sb("lr_lo", 188, [P, KD, P], F32R)
        glr = sb("glr", 192, [P, SEQ])
        gk2 = sb("gk2", 195, [LOWRANK, HEADS * DK])
        zabs = sb("zabs", 180, [P, HEADS, SEQ])
        sg_a = sb("sg_a", 176, [P, 2, SEQ])
        sg_b = sb("sg_b", 180, [P, 2, SEQ])
        prod_a = sb("prod_a", 184, [P, 2, SEQ])
        prod_b = sb("prod_b", 188, [P, 2, SEQ])
        sil = sb("sil", 176, [P, 2, SEQ])
        sgub_bc = sb("sgub_bc", 197, [P, GROUPS, P])
        swt = sb("swt", 201, [P, GROUPS, P])
        ident = sb("ident", 205, [P, P])
        ones_dv = sb("ones_dv", 205.5, [P, P])
        keep = sb("keep", 206, [P, SEQ], BF16)
        causal = sb("causal", 207, [P, P], U8)
        par = sb("par", 207.125, [P, K_END])
        small = sb("small", 207.375, [P, 24])
        ms, sd, rstd = small[:, 0:4], small[:, 4:8], small[:, 8:12]
        eps = small[:, 12:13]
        decay = small[:, 16:24]
        causal_f = sb("causal_f", 194.5, [P, P])
        bnst = sb("bnst", 194, [P, TT, 2, 6])
        bnag = sb("bnag", 194.25, [P, TT, 2])

        bank = [ctx.enter_context(nc.psum_tensor(f"bank{b}", [P, HALF], F32)) for b in range(8)]

        raw_landed = [sem(f"raw_landed{s}") for s in range(2)]
        hi_ready, lo_ready, block_used = sem("hi_ready"), sem("lo_ready"), sem("block_used")
        x_landed = [sem(f"x_landed{t}") for t in range(TT)]
        h_landed, fw_landed, lr_landed = sem("h_landed"), sem("fw_landed"), sem("lr_landed")
        par_landed, ident_landed, gk2_landed = sem("par_landed"), sem("ident_landed"), sem("gk2_landed")
        vbias_landed, ln_landed = sem("vbias_landed"), sem("ln_landed")
        sgub_landed, swt_landed, causal_landed = sem("sgub_landed"), sem("swt_landed"), sem("causal_landed")
        eps_set, keep_set, ones_set, sct_zeroed = sem("eps_set"), sem("keep_set"), sem("ones_set"), sem("sct_zeroed")
        causal_set = sem("causal_set")
        swt_masked = sem("swt_masked")
        sq_sum, sd_ready, rstd_ready, norm_ready = sem("sq_sum"), sem("sd_ready"), sem("rstd_ready"), sem("norm_ready")
        turned, turned_w, xt_hi_ready, xt_ready = sem("turned"), sem("turned_w"), sem("xt_hi_ready"), sem("xt_ready")
        lr_hi_ready, lr_lo_ready, lr_done, glr_ready = sem("lr_hi_ready"), sem("lr_lo_ready"), sem("lr_done"), sem("glr_ready")
        acc_done, acc_free = sem("acc_done"), sem("acc_free")
        tile_done, tile_free = sem("tile_done"), sem("tile_free")
        z_done, zabs_ready, zexp_ready, zln_ready, zmin_ready, g_ready = (
            sem("z_done"), sem("zabs_ready"), sem("zexp_ready"), sem("zln_ready"), sem("zmin_ready"), sem("g_ready"))
        vgelu_ready, bn_ready, bnag_ready, vsd_ready, vrstd_ready, vnorm_ready, vscaled, vn_ready = (
            sem("vgelu_ready"), sem("bn_ready"), sem("bnag_ready"), sem("vsd_ready"), sem("vrstd_ready"),
            sem("vnorm_ready"), sem("vscaled"), sem("vn_ready"))
        cum_ready, rest_ready, exp_ready, decayed = sem("cum_ready"), sem("rest_ready"), sem("exp_ready"), sem("decayed")
        staged, kend_turned, ken_ready = sem("staged"), sem("kend_turned"), sem("ken_ready")
        scores_done, sct_ready, kv_done, state_ready = sem("scores_done"), sem("sct_ready"), sem("kv_done"), sem("state_ready")
        mixed_done, mixed_biased, ya_ready = sem("mixed_done"), sem("mixed_biased"), sem("ya_ready")
        o_done, sq_ready, osq_ready, ms_done, osd_ready, orstd_ready, yb_scaled, yb_ready = (
            sem("o_done"), sem("sq_ready"), sem("osq_ready"), sem("ms_done"), sem("osd_ready"),
            sem("orstd_ready"), sem("yb_scaled"), sem("yb_ready"))
        y_hi_ready = sem("y_hi_ready")
        branch_done, branch_free, prod_ready, msum_ready, mg_hi_ready = (
            sem("branch_done"), sem("branch_free"), sem("prod_ready"), sem("msum_ready"), sem("mg_hi_ready"))
        gate_done, up_done, sil_ready, act_ready = sem("gate_done"), sem("up_done"), sem("sil_ready"), sem("act_ready")
        ah_ready, al_ready = sem("ah_ready"), sem("al_ready")
        y_ready, y_stored = sem("y_ready"), sem("y_stored")

        block = ctx.enter_context(nc.Block())

        def wk(t, s):
            return t[s][:, :].rearrange("p (k n) -> p k n", k=KD)

        def wn(t, s):
            return t[s][:, :].rearrange("p (k n) -> p k n", k=2)

        @block.sync
        def _(sp):
            for t in range(TT):
                sp.dma_start(xn_in[:, t, :], x[t * P:(t + 1) * P, :]).then_inc(x_landed[t], 16)
            for s in range(2):
                sp.dma_start(raw[s][:, :], wstream[s]).then_inc(raw_landed[s], 16)
            with sp.Fori(1, N_BLKS // 2) as i:
                for s in range(2):
                    sp.wait_ge(hi_ready, i * 2 + (s - 1))
                    sp.wait_ge(lo_ready, i * 2 + (s - 1))
                    sp.dma_start(raw[s][:, :], wstream[bass.ds(i * 2 + s, 1)].rearrange("a p n -> (a p) n")
                                 ).then_inc(raw_landed[s], 16)
            sp.wait_ge(hi_ready, N_BLKS - 2)
            sp.wait_ge(lo_ready, N_BLKS - 2)
            sp.dma_start(raw[0][:, :], wstream[N_BLKS - 1]).then_inc(raw_landed[0], 16)
            for t in range(TT):
                sp.wait_ge(y_ready, t + 1)
                sp.dma_start(out[t * P:(t + 1) * P, :], h[:, t, :]).then_inc(y_stored, 16)
            sp.wait_ge(y_stored, 16 * TT)

        @block.gpsimd
        def _(pool):
            pool.wait_ge(swt_landed, 16)
            pool.affine_select(out=swt[:, :, :], in_=swt[:, :, :], compare_op=ALU.is_ge, fill=0.0, base=0,
                               pattern=[[0, GROUPS], [1, P]], channel_multiplier=-1).then_inc(swt_masked, 1)

            def low(b, s, landed):
                pool.wait_ge(raw_landed[s], landed)
                pool.wait_ge(hi_ready, b + 1)
                pool.tensor_tensor(w_lo[s][:, :], raw[s][:, :], w_hi[s][:, :], ALU.subtract).then_inc(lo_ready, 1)

            with pool.Fori(0, N_BLKS // 2) as i:
                for s in range(2):
                    low(i * 2 + s, s, i * 16 + 16)
            low(N_BLKS - 1, 0, 16 * (N_BLKS // 2 + 1))

        @block.scalar
        def _(a):
            a.dma_start(lr_raw[:, :, :], w_lr).then_inc(lr_landed, 16)
            a.dma_start(par[:, :], cols).then_inc(par_landed, 16)
            a.dma_start(ident[:, :], ident_d).then_inc(ident_landed, 16)
            a.dma_start(vbias_bc[:, :, :].rearrange("p a n -> p (a n)"), vbias.partition_broadcast(P)).then_inc(vbias_landed, 16)
            a.dma_start(swt[:, :, :], sgu_wt).then_inc(swt_landed, 16)
            a.dma_start(gk2[:, :], w_gk2).then_inc(gk2_landed, 16)
            a.dma_start(lnw_bc[:, :], lnw.partition_broadcast(P)).then_inc(ln_landed, 16)
            a.dma_start(lnb_bc[:, :], lnb.partition_broadcast(P)).then_inc(ln_landed, 16)
            a.dma_start(sgub_bc[:, :, :].rearrange("p g t -> p (g t)"), sgub.partition_broadcast(P)).then_inc(sgub_landed, 16)
            a.dma_start(causal_f[:, :], causal_d).then_inc(causal_landed, 16)

            def high(b, s, landed):
                a.wait_ge(raw_landed[s], landed)
                a.activation(w_hi[s][:, :], raw[s][:, :], ACT.Copy).then_inc(hi_ready, 1)

            def high2(b, s, used, n):
                a.wait_ge(used, n)
                high(b, s, (b - s) * 8 + 16)

            def stats(src, t, junk, n0):
                a.activation(junk[:, :], src, ACT.Square, accum_out=ms[:, t:t + 1]).then_inc(sq_sum, 1)
                a.wait_ge(sq_sum, n0 + t + 1)
                a.activation(sd[:, t:t + 1], ms[:, t:t + 1], ACT.Sqrt, bias=eps, scale=1.0 / D).then_inc(sd_ready, 1)

            def split_turned(tmp, t, n0):
                for hf in range(2):
                    a.wait_ge(turned_w, n0 + 2 * t + hf + 1)
                    a.activation(xt_hi[:, 4 * hf:4 * hf + 4, t * P:(t + 1) * P], tmp[:, hf], ACT.Copy
                                 ).then_inc(xt_hi_ready, 1)

            a.wait_ge(eps_set, 1)
            for t in range(TT):
                a.wait_ge(x_landed[t], 16)
                stats(xn_in[:, t, :], t, sq_junk0, 0)
                if t == 1:
                    a.wait_ge(lr_landed, 16)
                    a.activation(lr_hi[:, :, :], lr_raw[:, :, :], ACT.Copy).then_inc(lr_hi_ready, 1)
                if t >= 1:
                    split_turned(xtmp, t - 1, 0)
                if t == 2:
                    high(0, 0, 16)
            split_turned(xtmp, TT - 1, 0)
            high(1, 1, 16)
            a.wait_ge(lr_done, 1)
            a.wait_ge(par_landed, 16)
            a.activation(glr[:, :], bank[7][:, :], ACT.Identity, bias=par[:, K_LR:K_LR + 1]).then_inc(glr_ready, 1)
            with a.Fori(0, 2) as i:
                for j in range(4):
                    if j < 3:
                        high2(i * 4 + (j + 2), j % 2, block_used, i * 3 + (j + 1))
                    else:
                        high2(i * 4 + (j + 2), j % 2, acc_done, i * 8 + 8)

            for hd in range(HEADS):
                a.wait_ge(z_done, hd + 1)
                a.activation(zabs[:, hd, :], bank[4 + hd][:, :], ACT.Abs, bias=par[:, K_BGK + hd:K_BGK + hd + 1]
                             ).then_inc(zabs_ready, 1)
            a.wait_ge(zabs_ready, HEADS)
            a.activation(zabs[:, :, :], zabs[:, :, :], ACT.Exp, scale=-1.0).then_inc(zexp_ready, 1)
            a.wait_ge(zexp_ready, 1)
            a.activation(zabs[:, :, :], zabs[:, :, :], ACT.Ln, bias=1.0).then_inc(zln_ready, 1)
            for t in range(TT):
                a.wait_ge(acc_free, 8 + 8 + 2 * t + 2)
                a.activation(vgs[:, 1, t, :], vgs[:, 1, t, :], ACT.Gelu_apprx_tanh).then_inc(vgelu_ready, 1)
            with a.Fori(0, 2) as i:
                for j in range(2):
                    for t in range(2):
                        n = 2 * j + t
                        a.wait_ge(tile_done, i * 4 + (n + 1))
                        a.activation(qk[:, bass.ds(i * 4 + n, 1), :], bank[n][:, :].unsqueeze(1), ACT.Identity,
                                     bias=par[:, bass.ds(i * 4 + (K_QK + n), 1)]).then_inc(tile_free, 1)
                    high2(i * 2 + (B_QK + 2 + j), j, tile_done, i * 4 + (2 * j + 2))
            a.wait_ge(bnag_ready, TT)
            a.activation(sd[:, :].unsqueeze(2), bnag[:, :, 1:2], ACT.Sqrt, bias=eps).then_inc(vsd_ready, 1)

            with a.Fori(0, HEADS) as i:
                def silu_r(t):
                    a.wait_ge(tile_done, i * 4 + (8 + t + 1))
                    a.activation(yb[:, bass.ds(i * 2 + t, 1), :], bank[t][:, :].unsqueeze(1), ACT.Silu,
                                 bias=par[:, bass.ds(i * 2 + (K_R + t), 1)]).then_inc(tile_free, 1)

                silu_r(0)
                a.wait_ge(cum_ready, i + 1)
                a.activation(expb[:, :, :], cum[:, :, :], ACT.Exp, scale=1.0 / GATE_NORM).then_inc(exp_ready, 1)
                a.wait_ge(rest_ready, i + 1)
                a.activation(rest[:, :, :], rest[:, :, :], ACT.Exp, scale=1.0 / GATE_NORM).then_inc(exp_ready, 1)
                a.activation(cum[:, :, :], cum[:, :, :], ACT.Exp, scale=-1.0 / GATE_NORM).then_inc(exp_ready, 1)
                a.wait_ge(vn_ready, 2 * TT)
                a.activation(vst[:, :, :], vgs[:, 0, :, bass.ds(i * DV, DV)], ACT.Copy).then_inc(staged, 1)
                a.activation(vns[:, :, :], vgs[:, 1, :, bass.ds(i * DV, DV)], ACT.Copy).then_inc(staged, 1)
                silu_r(1)
                high2(i * 2 + (B_RU + 2), 0, tile_done, i * 4 + 10)
                a.wait_ge(tile_done, i * 4 + 11)
                a.activation(ya[:, bass.ds(i * 2, 1), :], bank[0][:, :].unsqueeze(1), ACT.Gelu_apprx_tanh,
                             bias=par[:, bass.ds(i * 2 + K_U, 1)]).then_inc(tile_free, 1)
                a.wait_ge(kend_turned, i + 1)
                a.activation(ken[:, :, :], bank[4][:, :], ACT.Copy).then_inc(ken_ready, 1)
                a.wait_ge(tile_done, i * 4 + 12)
                a.activation(ya[:, bass.ds(i * 2 + 1, 1), :], bank[1][:, :].unsqueeze(1), ACT.Gelu_apprx_tanh,
                             bias=par[:, bass.ds(i * 2 + (K_U + 1), 1)]).then_inc(tile_free, 1)
                high2(i * 2 + (B_RU + 3), 1, tile_done, i * 4 + 12)
                a.wait_ge(o_done, i * 2 + 1)
                a.activation(osq[:, :], bank[6][:, :], ACT.Square).then_inc(sq_ready, 1)
                a.wait_ge(o_done, i * 2 + 2)
                a.activation(rs[:, :], bank[7][:, :], ACT.Square).then_inc(sq_ready, 1)
                a.wait_ge(ms_done, i + 1)
                a.activation(rs[:, :], bank[2][:, :], ACT.Sqrt, bias=eps).then_inc(osd_ready, 1)

            a.wait_ge(ya_ready, KD)
            for q in range(2):
                a.activation(ya_hi[:, 4 * q:4 * q + 4, :], ya[:, 4 * q:4 * q + 4, :], ACT.Copy).then_inc(y_hi_ready, 1)
            for q in range(2):
                a.wait_ge(yb_ready, 4 * q + 4)
                a.activation(yb_hi[:, 4 * q:4 * q + 4, :], yb[:, 4 * q:4 * q + 4, :], ACT.Copy).then_inc(y_hi_ready, 1)
            with a.Fori(0, KD // 2) as i:
                for j, (sg, kc) in enumerate(((sg_a, K_GA), (sg_b, K_GB))):
                    for t in range(2):
                        a.wait_ge(tile_done, i * 4 + (24 + 2 * j + t + 1))
                        a.wait_ge(branch_free, i * 2 + 1)
                        a.activation(sg[:, t, :], bank[2 * j + t][:, :], ACT.Sigmoid,
                                     bias=par[:, bass.ds(i * 2 + (kc + t), 1)]).then_inc(tile_free, 1)
                    high2(i * 4 + (B_MERGE + 2 + j), j, tile_done, i * 4 + (24 + 2 * j + 2))
                high2(i * 4 + (B_MERGE + 4), 0, branch_done, i * 4 + 2)
                high2(i * 4 + (B_MERGE + 5), 1, branch_done, i * 4 + 4)
                for t in range(2):
                    a.wait_ge(msum_ready, i * 2 + (t + 1))
                    a.activation(mg_hi[:, bass.ds(i * 2 + t, 1), :], prod_a[:, t:t + 1, :], ACT.Copy
                                 ).then_inc(mg_hi_ready, 1)

            a.wait_ge(branch_done, 2 * KD)
            a.dma_start(h[:, :, :], x.rearrange("(t p) n -> p t n", p=P)).then_inc(h_landed, 16)
            a.dma_start(fw[:, :], finalw.partition_broadcast(P)).then_inc(fw_landed, 16)
            for j in range(3):
                high2(B_OUT + 2 + j, j % 2, block_used, 6 + j + 1)
            for t in range(TT):
                a.wait_ge(acc_free, 24 + 2 * t + 2)
                stats(h[:, t, :], t, sq_junk, TT)
                if t >= 1:
                    split_turned(htmp, t - 1, 8)
            high2(B_FFN + 1, 1, acc_done, 24)
            split_turned(htmp, TT - 1, 8)

            def gates(i, first=False):
                for t in range(2):
                    a.wait_ge(gate_done, i * 2 + (t + 1))
                    if not first:
                        a.wait_ge(act_ready, i * 2 + (t - 1))
                    a.activation(sil[:, t, :], bank[t][:, :], ACT.Silu).then_inc(sil_ready, 1)
                high2(i * 2 + (B_FFN + 2), 0, gate_done, i * 2 + 2)
                high2(i * 2 + (B_FFN + 3), 1, up_done, i * 2 + 2)

            def act_high(m, s):
                a.activation(ah[s][:, :, :], act[:, bass.ds(m * 2, 2), :], ACT.Copy).then_inc(ah_ready, 1)

            gates(0, True)
            a.wait_ge(act_ready, 2)
            act_high(0, 0)
            with a.Fori(1, FFN_IT) as i:
                gates(i)
            act_high(1, 1)
            high2(B_DOWN + 2, 0, block_used, 9 + 1)
            a.wait_ge(act_ready, KF)
            act_high(2, 0)
            with a.Fori(0, 4) as i:
                for s in range(2):
                    high2(i * 2 + (B_DOWN + 3 + s), 1 - s, block_used, i * 2 + (9 + 2 + s))
                    act_high(i * 2 + (3 + s), 1 - s)
            for t in range(TT):
                a.wait_ge(acc_free, 32 + 2 * t + 2)
                stats(h[:, t, :], t, sq_junk2, 2 * TT)

        @block.vector
        def _(v):
            v.memset(eps, EPS).then_inc(eps_set, 1)
            v.memset(keep[:, :], 1.0).then_inc(keep_set, 1)
            v.memset(ones_dv[:, :], 1.0 / DV).then_inc(ones_set, 1)
            v.memset(sct[:, :, :], 0.0).then_inc(sct_zeroed, 1)
            v.wait_ge(keep_set, 1)
            v.memset(keep[:, :].rearrange("p (c t) -> p c t", t=CHUNK)[:, :, 0:1], 0.0).then_inc(keep_set, 1)
            v.wait_ge(par_landed, 16)

            def normalise(dst, src, t, n0):
                v.wait_ge(sd_ready, n0 + t + 1)
                v.reciprocal(rstd[:, t:t + 1], sd[:, t:t + 1]).then_inc(rstd_ready, 1)
                v.wait_ge(rstd_ready, n0 + t + 1)
                if t >= 2:
                    v.wait_ge(turned, 2 * (n0 + t - 1))
                v.tensor_scalar(dst, src, rstd[:, t:t + 1], None, ALU.mult).then_inc(norm_ready, 1)

            def split_turned(tmp, t, n0, kw):
                for hf in range(2):
                    n = n0 + 2 * t + hf
                    v.wait_ge(turned, n + 1)
                    if n >= 2:
                        v.wait_ge(xt_ready, n - 1)
                    w = par[:, kw + 4 * hf:kw + 4 * hf + 4].unsqueeze(2).broadcast_to([P, 4, P])
                    v.tensor_tensor(tmp[:, hf], bank[2 * t + hf][:, :].rearrange("p (k t) -> p k t", k=4), w, ALU.mult
                                    ).then_inc(turned_w, 1)
                for hf in range(2):
                    n = n0 + 2 * t + hf
                    v.wait_ge(xt_hi_ready, n + 1)
                    v.tensor_tensor(xt_lo[:, 4 * hf:4 * hf + 4, t * P:(t + 1) * P], tmp[:, hf],
                                    xt_hi[:, 4 * hf:4 * hf + 4, t * P:(t + 1) * P], ALU.subtract).then_inc(xt_ready, 1)

            normalise(xnat[:, 0, :], xn_in[:, 0, :], 0, 0)
            for t in range(1, TT):
                normalise(xnat[:, t % 2, :], xn_in[:, t, :], t, 0)
                split_turned(xtmp, t - 1, 0, K_N1)
                if t == 1:
                    v.wait_ge(lr_hi_ready, 1)
                    v.tensor_tensor(lr_lo[:, :, :], lr_raw[:, :, :], lr_hi[:, :, :], ALU.subtract).then_inc(lr_lo_ready, 1)
            split_turned(xtmp, TT - 1, 0, K_N1)

            v.wait_ge(causal_landed, 16)
            v.tensor_copy(causal[:, :], causal_f[:, :]).then_inc(causal_set, 1)
            v.wait_ge(vbias_landed, 16)
            with v.Fori(0, 2) as i:
                for t in range(TT):
                    for hf in range(2):
                        v.wait_ge(acc_done, i * 8 + (2 * t + hf + 1))
                        cs = slice(hf * HALF, (hf + 1) * HALF)
                        v.tensor_tensor(vgs[:, bass.ds(i, 1), t, cs], bank[2 * t + hf][:, :].unsqueeze(1),
                                        vbias_bc[:, bass.ds(i, 1), cs], ALU.add).then_inc(acc_free, 1)

            for hd in range(HEADS):
                v.wait_ge(zabs_ready, hd + 1)
                v.tensor_scalar(g[:, hd, :], bank[4 + hd][:, :], par[:, K_BGK + hd:K_BGK + hd + 1], 0.0,
                                ALU.add, ALU.min).then_inc(zmin_ready, 1)
            v.wait_ge(zln_ready, 1)
            v.wait_ge(zmin_ready, HEADS)
            v.tensor_tensor(g[:, :, :], g[:, :, :], zabs[:, :, :], ALU.subtract).then_inc(g_ready, 1)

            for t in range(TT):
                v.wait_ge(vgelu_ready, t + 1)
                for hf in range(2):
                    v.bn_stats(bnst[:, t, hf, :], vgs[:, 1, t, hf * HALF:(hf + 1) * HALF]).then_inc(bn_ready, 1)
                v.wait_ge(bn_ready, 2 * t + 2)
                v.bn_aggr(bnag[:, t, :], bnst[:, t, :, :]).then_inc(bnag_ready, 1)
            v.wait_ge(vsd_ready, 1)
            v.reciprocal(rstd[:, :], sd[:, :]).then_inc(vrstd_ready, 1)
            v.wait_ge(vrstd_ready, 1)
            v.wait_ge(ln_landed, 32)
            for t in range(TT):
                v.tensor_scalar(vgs[:, 1, t, :], vgs[:, 1, t, :], bnag[:, t, 0:1], rstd[:, t:t + 1],
                                ALU.subtract, ALU.mult).then_inc(vnorm_ready, 1)
            for t in range(TT):
                v.wait_ge(vnorm_ready, t + 1)
                v.tensor_tensor(vgs[:, 1, t, :], vgs[:, 1, t, :], lnw_bc[:, :], ALU.mult).then_inc(vscaled, 1)
            for t in range(TT):
                v.wait_ge(vscaled, t + 1)
                v.tensor_tensor(vgs[:, 1, t, :], vgs[:, 1, t, :], lnb_bc[:, :], ALU.add).then_inc(vn_ready, 2)

            v.wait_ge(g_ready, 1)
            v.wait_ge(keep_set, 2)
            v.wait_ge(sct_zeroed, 1)
            v.wait_ge(sgub_landed, 16)
            v.wait_ge(causal_set, 1)
            with v.Fori(0, HEADS) as i:
                v.tensor_tensor_scan(cum[:, :, :].rearrange("p c t -> p (c t)"), keep[:, :],
                                     g[:, bass.ds(i, 1), :].rearrange("p a t -> p (a t)"), 0.0,
                                     ALU.mult, ALU.add).then_inc(cum_ready, 1)
                v.wait_ge(cum_ready, i + 1)
                v.tensor_tensor(rest[:, :, :], cum[:, :, CHUNK - 1:CHUNK].broadcast_to([P, NCH, CHUNK]), cum[:, :, :],
                                ALU.subtract).then_inc(rest_ready, 1)
                v.wait_ge(exp_ready, i * 3 + 1)
                v.wait_ge(tile_free, 4 + 8)
                v.tensor_copy(decay.unsqueeze(2), expb[:, :, CHUNK - 1:CHUNK]).then_inc(decayed, 1)
                v.wait_ge(decayed, i * 4 + 1)
                v.scalar_tensor_tensor(expb[:, :, :].rearrange("p c t -> p (c t)"),
                                       qk[:, bass.ds(i, 1), :].rearrange("p a t -> p (a t)"), DK ** -0.5,
                                       expb[:, :, :].rearrange("p c t -> p (c t)"), ALU.mult, ALU.mult).then_inc(decayed, 1)
                v.wait_ge(exp_ready, i * 3 + 2)
                kh = qk[:, bass.ds(i + HEADS, 1), :].rearrange("p a (c t) -> p (a c) t", t=CHUNK)
                v.tensor_tensor(rest[:, :, :], kh, rest[:, :, :], ALU.mult).then_inc(decayed, 1)
                v.wait_ge(exp_ready, i * 3 + 3)
                v.tensor_tensor(cum[:, :, :], kh, cum[:, :, :], ALU.mult).then_inc(decayed, 1)

                for n in range(NCH - 1):
                    if n % 2 == 0:
                        v.wait_ge(kv_done, i * 4 + (n // 2 + 1))
                    kv = bank[KV_BANKS[n % 4]][:, 0:DV]
                    if n == 0:
                        v.wait_ge(scores_done, i + 1)
                        v.tensor_copy(state[:, 0, :], kv).then_inc(state_ready, 1)
                    else:
                        v.wait_ge(state_ready, i * 7 + n)
                        v.scalar_tensor_tensor(state[:, n, :], state[:, n - 1, :], decay[:, n:n + 1], kv,
                                               ALU.mult, ALU.add).then_inc(state_ready, 1)
                    if n == 1:
                        v.copy_predicated(sct[:, :, :], causal[:, :].unsqueeze(1).broadcast_to([P, TT, P]),
                                          bank[5][:, :].rearrange("p (t s) -> p t s", t=TT)).then_inc(sct_ready, 1)

                def gate_mixed(q):
                    v.wait_ge(mixed_done, i * 2 + (q + 1))
                    m = bank[4 - q][:, :].rearrange("p (n t) -> p n t", n=TT)
                    v.tensor_tensor(m, m, sgub_bc[:, bass.ds(i * 2 + q, 1), :].broadcast_to([P, TT, P]), ALU.add
                                    ).then_inc(mixed_biased, 1)
                    v.wait_ge(mixed_biased, i * 2 + (q + 1))
                    v.wait_ge(tile_free, i * 4 + (4 + 8 + 3 + q))
                    yg = ya[:, bass.ds(i * 2 + q, 1), :].rearrange("p a t -> p (a t)")
                    v.tensor_tensor(yg, yg, bank[4 - q][:, :], ALU.mult).then_inc(ya_ready, 1)

                gate_mixed(0)
                v.wait_ge(sq_ready, i * 2 + 2)
                v.tensor_tensor(osq[:, :], osq[:, :], rs[:, :], ALU.add).then_inc(osq_ready, 1)
                gate_mixed(1)
                for q in range(2):
                    yh = yb[:, bass.ds(i * 2 + q, 1), :].rearrange("p a t -> p (a t)")
                    v.scalar_tensor_tensor(yh, bank[6 + q][:, :], par[:, K_GN + q:K_GN + q + 1], yh, ALU.mult, ALU.mult
                                           ).then_inc(yb_scaled, 1)
                v.wait_ge(osd_ready, i + 1)
                v.reciprocal(rs[:, :], rs[:, :]).then_inc(orstd_ready, 1)
                v.wait_ge(orstd_ready, i + 1)
                v.wait_ge(yb_scaled, i * 2 + 2)
                for q in range(2):
                    yh = yb[:, bass.ds(i * 2 + q, 1), :].rearrange("p a t -> p (a t)")
                    v.tensor_tensor(yh, yh, rs[:, :], ALU.mult).then_inc(yb_ready, 1)

            for q in range(2):
                ks = slice(4 * q, 4 * q + 4)
                v.wait_ge(y_hi_ready, q + 1)
                v.tensor_tensor(ya_lo[:, ks, :], ya[:, ks, :], ya_hi[:, ks, :], ALU.subtract)
            v.wait_ge(y_hi_ready, 3)
            v.tensor_tensor(yb_lo[:, 0:4, :], yb[:, 0:4, :], yb_hi[:, 0:4, :], ALU.subtract)
            v.wait_ge(y_hi_ready, 4)
            v.tensor_tensor(yb_lo[:, 4:8, :], yb[:, 4:8, :], yb_hi[:, 4:8, :], ALU.subtract).then_inc(branch_free, 1)

            with v.Fori(0, KD // 2) as i:
                v.wait_ge(tile_free, i * 4 + (4 + 24 + 4))
                for q in range(2):
                    v.wait_ge(branch_done, i * 4 + (q + 1))
                    v.tensor_tensor(prod_a[:, q, :], bank[4 + q][:, :], sg_a[:, q, :], ALU.mult).then_inc(prod_ready, 1)
                for q in range(2):
                    v.wait_ge(branch_done, i * 4 + (q + 3))
                    v.tensor_tensor(prod_b[:, q, :], bank[6 + q][:, :], sg_b[:, q, :], ALU.mult).then_inc(prod_ready, 1)
                for q in range(2):
                    v.wait_ge(prod_ready, i * 4 + (q + 3))
                    v.tensor_tensor(prod_a[:, q, :], prod_a[:, q, :], prod_b[:, q, :], ALU.add).then_inc(msum_ready, 1)
                for q in range(2):
                    v.wait_ge(mg_hi_ready, i * 2 + (q + 1))
                    v.tensor_tensor(mg_lo[:, bass.ds(i * 2 + q, 1), :], prod_a[:, q:q + 1, :],
                                    mg_hi[:, bass.ds(i * 2 + q, 1), :], ALU.subtract).then_inc(branch_free, 1)

            def residual(t, n0):
                for hf in range(2):
                    v.wait_ge(acc_done, n0 + 2 * t + hf + 1)
                    hs = h[:, t, hf * HALF:(hf + 1) * HALF]
                    v.tensor_tensor(hs, bank[2 * t + hf][:, :], hs, ALU.add).then_inc(acc_free, 1)

            v.wait_ge(h_landed, 16)
            residual(0, 16)
            normalise(hn[:, 0, :], h[:, 0, :], 0, TT)
            for t in range(1, TT):
                residual(t, 16)
                split_turned(htmp, t - 1, 8, K_N2)
                normalise(hn[:, t % 2, :], h[:, t, :], t, TT)
            split_turned(htmp, TT - 1, 8, K_N2)

            def gated(i):
                for t in range(2):
                    v.wait_ge(sil_ready, i * 2 + (t + 1))
                    v.wait_ge(up_done, i * 2 + (t + 1))
                    v.tensor_tensor(act[:, bass.ds(i * 2 + t, 1), :], bank[2 + t][:, :].unsqueeze(1),
                                    sil[:, t:t + 1, :], ALU.mult).then_inc(act_ready, 1)

            def act_low(m, s):
                v.wait_ge(ah_ready, m + 1)
                v.tensor_tensor(al[s][:, :, :], act[:, bass.ds(m * 2, 2), :], ah[s][:, :, :], ALU.subtract
                                ).then_inc(al_ready, 1)

            gated(0)
            act_low(0, 0)
            with v.Fori(1, FFN_IT) as i:
                gated(i)
            act_low(1, 1)
            act_low(2, 0)
            with v.Fori(0, 4) as i:
                for s in range(2):
                    act_low(i * 2 + (3 + s), 1 - s)
            v.wait_ge(fw_landed, 16)
            for t in range(TT):
                residual(t, 24)
                v.wait_ge(sd_ready, 2 * TT + t + 1)
                v.reciprocal(rstd[:, t:t + 1], sd[:, t:t + 1]).then_inc(rstd_ready, 1)
                v.wait_ge(rstd_ready, 2 * TT + t + 1)
                v.scalar_tensor_tensor(h[:, t, :], h[:, t, :], rstd[:, t:t + 1], fw[:, :], ALU.mult, ALU.mult
                                       ).then_inc(y_ready, 1)

        @block.tensor
        def _(pe):
            def turn(src, dst0, t, n0):
                pe.wait_ge(norm_ready, n0 + t + 1)
                for hf in range(2):
                    for k in range(4):
                        c = (4 * hf + k) * P
                        last = pe.transpose(bank[dst0 + hf][:, k * P:(k + 1) * P], src[:, c:c + P], ident[:, :])
                    last.then_inc(turned, 1)

            def arrived(b):
                pe.wait_ge(hi_ready, b + 1)
                pe.wait_ge(lo_ready, b + 1)

            def tile_T(dst, wh, wl, t, rh, rl, ts=slice(0, SEQ)):
                cs = slice(t * P, (t + 1) * P)
                for k in range(KD):
                    pe.matmul(dst, wh[:, k, cs], rh[:, k, ts], start=(k == 0), stop=False)
                    pe.matmul(dst, wh[:, k, cs], rl[:, k, ts], start=False, stop=False)
                    last = pe.matmul(dst, wl[:, k, cs], rh[:, k, ts], start=False, stop=(k == KD - 1))
                return last

            def block_N(s, lh, ll, first, last, before=None, after=None):
                wh, wl = wn(w_hi, s), wn(w_lo, s)
                for t in range(TT):
                    if before is not None:
                        before(t)
                    for hf in range(2):
                        cs = slice(hf * HALF, (hf + 1) * HALF)
                        for k in range(2):
                            ts = slice(t * P, (t + 1) * P)
                            dst = bank[2 * t + hf][:, :]
                            pe.matmul(dst, lh[:, k, ts], wh[:, k, cs], start=(first and k == 0), stop=False)
                            pe.matmul(dst, lh[:, k, ts], wl[:, k, cs], start=False, stop=False)
                            mm = pe.matmul(dst, ll[:, k, ts], wh[:, k, cs], start=False, stop=(last and k == 1))
                        if last:
                            mm.then_inc(acc_done, 1)
                    if after is not None:
                        after(t)
                if not last:
                    mm.then_inc(block_used, 1)

            pe.wait_ge(ident_landed, 16)
            for t in range(TT):
                turn(xnat[:, t % 2, :], 2 * t, t, 0)
            pe.wait_ge(lr_lo_ready, 1)
            pe.wait_ge(xt_ready, 2 * TT)
            tile_T(bank[7][:, :], lr_hi, lr_lo, 0, xt_hi, xt_lo).then_inc(lr_done, 1)
            pe.sem_inc(acc_free, 8)
            with pe.Fori(0, 2) as i:
                for j in range(4):
                    arrived(i * 4 + j)

                    def free(t):
                        if j == 0:
                            pe.wait_ge(acc_free, i * 8 + (2 * t + 2))
                            if t == TT - 1:
                                pe.wait_ge(glr_ready, 1)
                    ks = slice(2 * j, 2 * j + 2)
                    block_N(j % 2, xt_hi[:, ks, :], xt_lo[:, ks, :], j == 0, j == 3, free)

            pe.wait_ge(acc_free, 8 + 16)
            pe.wait_ge(gk2_landed, 16)
            for hd in range(HEADS):
                pe.matmul(bank[4 + hd][:, :], gk2[:, hd * DK:(hd + 1) * DK], glr[0:LOWRANK, :], start=True, stop=True
                          ).then_inc(z_done, 1)
            pe.sem_inc(tile_free, 4)
            with pe.Fori(0, 2) as i:
                for j in range(2):
                    arrived(i * 2 + (B_QK + j))
                    for t in range(2):
                        n = 2 * j + t
                        pe.wait_ge(tile_free, i * 4 + (n + 1))
                        mm = tile_T(bank[n][:, :], wk(w_hi, j), wk(w_lo, j), t, xt_hi, xt_lo).then_inc(tile_done, 1)

            pe.wait_ge(ones_set, 1)
            pe.wait_ge(swt_masked, 1)
            with pe.Fori(0, HEADS) as i:
                def gate_tile(j, t):
                    n = 2 * j + t
                    pe.wait_ge(tile_free, i * 4 + (8 + n + 3))
                    tile_T(bank[t][:, :], wk(w_hi, j), wk(w_lo, j), t, xt_hi, xt_lo).then_inc(tile_done, 1)

                def mix(q):
                    w = swt[:, bass.ds(i * 2 + q, 1), :].rearrange("p a t -> p (a t)")
                    for n in range(TT):
                        mm = pe.matmul(bank[4 - q][:, n * P:(n + 1) * P], vns[:, n, q * P:(q + 1) * P], w,
                                       start=True, stop=True)
                    mm.then_inc(mixed_done, 1)

                arrived(i * 2 + B_RU)
                gate_tile(0, 0)
                gate_tile(0, 1)
                arrived(i * 2 + (B_RU + 1))
                gate_tile(1, 0)
                pe.wait_ge(decayed, i * 4 + 4)
                for t in range(TT):
                    mm = pe.transpose(bank[4][:, t * P:(t + 1) * P], rest[:, 2 * t:2 * t + 2, :].rearrange("p c t -> p (c t)"),
                                      ident[:, :])
                mm.then_inc(kend_turned, 1)
                for t in range(TT):
                    mm = pe.matmul(bank[5][:, t * P:(t + 1) * P], cum[:, 2 * t:2 * t + 2, :].rearrange("p c t -> p (c t)"),
                                   expb[:, 2 * t:2 * t + 2, :].rearrange("p c t -> p (c t)"), start=True, stop=True)
                mm.then_inc(scores_done, 1)
                gate_tile(1, 1)
                pe.wait_ge(ken_ready, i + 1)
                pe.wait_ge(staged, i * 2 + 2)
                for n in range(NCH - 1):
                    if n in (4, 6):
                        pe.wait_ge(state_ready, i * 7 + (n - 2))
                    r0 = (n % 2) * CHUNK
                    mm = pe.matmul(bank[KV_BANKS[n % 4]][:, 0:DV],
                                   ken[r0:r0 + CHUNK, n // 2, :], vst[r0:r0 + CHUNK, n // 2, :], start=True, stop=True)
                    if n % 2 == 1 or n == NCH - 2:
                        mm.then_inc(kv_done, 1)
                mix(0)
                pe.wait_ge(sct_ready, i + 1)
                pe.wait_ge(state_ready, i * 7 + 7)
                for q in range(2):
                    qs = slice(q * P, (q + 1) * P)
                    for t in range(TT):
                        pe.matmul(bank[6 + q][:, t * P:(t + 1) * P], vst[:, t, qs], sct[:, t, :],
                                  start=(t == 0), stop=(t == 0), skip_group_check=True)
                        for n in (2 * t, 2 * t + 1):
                            if n > 0:
                                mm = pe.matmul(bank[6 + q][:, n * CHUNK:(n + 1) * CHUNK], state[:, n - 1, qs], expb[:, n, :],
                                               start=False, stop=True, skip_group_check=True)
                    mm.then_inc(o_done, 1)
                mix(1)
                pe.wait_ge(osq_ready, i + 1)
                pe.matmul(bank[2][:, :], ones_dv[:, :], osq[:, :], start=True, stop=True).then_inc(ms_done, 1)

            pe.wait_ge(tile_free, 4 + 24)
            with pe.Fori(0, KD // 2) as i:
                for j in range(2):
                    arrived(i * 4 + (B_MERGE + j))
                    for t in range(2):
                        n = 2 * j + t
                        pe.wait_ge(tile_free, i * 4 + (24 + n + 1))
                        if n == 2:
                            pe.wait_ge(yb_ready, KD)
                        tile_T(bank[n][:, :], wk(w_hi, j), wk(w_lo, j), t, xt_hi, xt_lo).then_inc(tile_done, 1)
                pe.wait_ge(branch_free, i * 2 + 1)
                for j, (yh, yl) in enumerate(((ya_hi, ya_lo), (yb_hi, yb_lo))):
                    arrived(i * 4 + (B_MERGE + 2 + j))
                    for t in range(2):
                        tile_T(bank[4 + 2 * j + t][:, :], wk(w_hi, j), wk(w_lo, j), t, yh, yl).then_inc(branch_done, 1)

            pe.wait_ge(tile_free, 4 + 40)
            for j in range(4):
                arrived(B_OUT + j)
                pe.wait_ge(branch_free, 2 * j + 3)
                if j == 0:
                    pe.wait_ge(branch_free, 1 + KD)
                ks = slice(2 * j, 2 * j + 2)

                def turn_before(t):
                    if j == 3 and t >= 1:
                        turn(hn[:, (t - 1) % 2, :], 2 * (t - 1), t - 1, TT)
                block_N(j % 2, mg_hi[:, ks, :], mg_lo[:, ks, :], j == 0, j == 3, None, turn_before)

            s0, s1 = slice(0, SEQ // 2), slice(SEQ // 2, SEQ)
            arrived(B_FFN)
            pe.wait_ge(xt_ready, 8 + 4)
            for t in range(2):
                tile_T(bank[t][:, s0], wk(w_hi, 0), wk(w_lo, 0), t, xt_hi, xt_lo, s0)
            turn(hn[:, 1, :], 6, 3, TT)
            arrived(B_FFN + 1)
            for t in range(2):
                tile_T(bank[2 + t][:, s0], wk(w_hi, 1), wk(w_lo, 1), t, xt_hi, xt_lo, s0)
            pe.wait_ge(xt_ready, 16)
            for t in range(2):
                tile_T(bank[t][:, s1], wk(w_hi, 0), wk(w_lo, 0), t, xt_hi, xt_lo, s1).then_inc(gate_done, 1)
            for t in range(2):
                tile_T(bank[2 + t][:, s1], wk(w_hi, 1), wk(w_lo, 1), t, xt_hi, xt_lo, s1).then_inc(up_done, 1)
            with pe.Fori(1, FFN_IT) as i:
                arrived(i * 2 + B_FFN)
                for t in range(2):
                    pe.wait_ge(sil_ready, i * 2 + (t - 1))
                    tile_T(bank[t][:, :], wk(w_hi, 0), wk(w_lo, 0), t, xt_hi, xt_lo).then_inc(gate_done, 1)
                arrived(i * 2 + (B_FFN + 1))
                for t in range(2):
                    pe.wait_ge(act_ready, i * 2 + (t - 1))
                    tile_T(bank[2 + t][:, :], wk(w_hi, 1), wk(w_lo, 1), t, xt_hi, xt_lo).then_inc(up_done, 1)

            def down(m, s, first=False, last=False):
                arrived(m + B_DOWN)
                pe.wait_ge(al_ready, m + 1)

                def free(t):
                    if first and t == 0:
                        pe.wait_ge(sil_ready, KF)
                    if first and t == 1:
                        pe.wait_ge(act_ready, KF)
                block_N(s, ah[s], al[s], first, last, free)

            down(0, 0, first=True)
            with pe.Fori(0, 4) as i:
                down(i * 2 + 1, 1)
                down(i * 2 + 2, 0)
            down(DOWN_BLKS - 2, 1)
            down(DOWN_BLKS - 1, 0, last=True)


def _t_block(w, c0):
    return w[:, c0:c0 + 256].reshape(KD, P, 256).transpose(1, 0, 2).reshape(P, BLK)


def _n_block(w, j, c0=0):
    return w[256 * j:256 * (j + 1), c0:c0 + D].reshape(2, P, D).transpose(1, 0, 2).reshape(P, BLK)


def _tiles(v):
    return v.reshape(-1, P).T


def kernel(x, norm1_w, w_in, b_in, sgu_ln_w, sgu_ln_b, sgu_w, sgu_b, w_gk2, b_gk, gla_norm_w,
           w_branch_a, w_branch_b, w_out, norm2_w, w_ffn_gate, w_ffn_up, w_ffn_down, final_norm_w):
    import concourse.bacc as bacc
    from concourse.bass_utils import run_bass_kernel_spmd

    f = np.asarray
    x2, wi, bi = f(x)[0], f(w_in)[0], f(b_in)[0]
    wa, wb, wo = f(w_branch_a)[0], f(w_branch_b)[0], f(w_out)[0]
    wg, wu, wd = f(w_ffn_gate)[0], f(w_ffn_up)[0], f(w_ffn_down)[0]

    blocks = [_n_block(wi, j, C_VG) for j in range(4)] + [_n_block(wi, j, C_V) for j in range(4)]
    blocks += [_t_block(wi, C_Q + 256 * j) for j in range(4)]
    for i in range(4):
        blocks += [_t_block(wi, C_R + 256 * i), _t_block(wi, C_U + 256 * i)]
    for i in range(4):
        blocks += [_t_block(wi, C_GA + 256 * i), _t_block(wi, C_GB + 256 * i),
                   _t_block(wa, 256 * i), _t_block(wb, 256 * i)]
    blocks += [_n_block(wo, j) for j in range(4)]
    for i in range(FFN_IT):
        blocks += [_t_block(wg, 256 * i), _t_block(wu, 256 * i)]
    blocks += [_n_block(wd, j) for j in range(DOWN_BLKS)]

    cols = np.concatenate([
        _tiles(bi[C_Q:C_Q + D]), _tiles(bi[C_LR:C_LR + P]), _tiles(bi[C_R:C_R + D]), _tiles(bi[C_U:C_U + D]),
        _tiles(bi[C_GA:C_GA + D]), _tiles(bi[C_GB:C_GB + D]), _tiles(f(b_gk)[0]), _tiles(f(gla_norm_w)[0]),
        _tiles(f(norm1_w)[0]), _tiles(f(norm2_w)[0])], axis=1)
    tok = np.arange(P)
    causal = ((tok[:, None] <= tok[None, :]) & (tok[:, None] // CHUNK == tok[None, :] // CHUNK)).astype(np.float32)

    arrays = {
        "x": x2,
        "wstream": np.stack(blocks),
        "w_lr": wi[:, C_LR:C_LR + P].reshape(KD, P, P).transpose(1, 0, 2),
        "cols": cols,
        "vbias": np.concatenate([bi[C_VG:C_VG + D], bi[C_V:C_V + D]]),
        "lnw": f(sgu_ln_w)[0], "lnb": f(sgu_ln_b)[0],
        "sgub": f(sgu_b)[0].reshape(-1),
        "sgu_wt": f(sgu_w)[0].transpose(2, 0, 1),
        "w_gk2": f(w_gk2)[0],
        "ident_d": np.eye(P, dtype=np.float32),
        "causal_d": causal,
        "finalw": f(final_norm_w),
    }
    nc = bacc.Bacc("TRN2", target_bir_lowering=False, num_devices=1)
    arrays = {k: np.ascontiguousarray(a) for k, a in arrays.items()}
    aps = {k: nc.dram_tensor(k, a.shape, mybir.dt.from_np(a.dtype), kind="ExternalInput").ap() for k, a in arrays.items()}
    aps["out"] = nc.dram_tensor("out", (SEQ, D), F32, kind="ExternalOutput").ap()
    build(nc, **aps)
    r = run_bass_kernel_spmd(nc, [arrays], core_ids=[0])
    return r.results[0]["out"].reshape(1, SEQ, D)
```

```python
from contextlib import ExitStack

import numpy as np

import concourse.bass as bass
from concourse import mybir

ALU = mybir.AluOpType
ACT = mybir.ActivationFunctionType
F32 = mybir.dt.float32
F32R = mybir.dt.float32r
BF16 = mybir.dt.bfloat16
U8 = mybir.dt.uint8

P = 128
SEQ = 512
D = 1024
TT = SEQ // P
KD = D // P
HEADS = 4
DK = 128
DV = 256
CHUNK = 64
NCH = SEQ // CHUNK
GROUPS = 8
LOWRANK = 16
DFF = 2816
KF = DFF // P
EPS = 1e-6
GATE_NORM = 16.0
KV_BANKS = (2, 3, 4, 5)
BLK = 2048
HALF = 512

C_U, C_V, C_Q, C_K, C_VG, C_R, C_LR, C_GA, C_GB = 0, 1024, 2048, 2560, 3072, 4096, 5120, 5136, 6160

B_VG = 0
B_QK = 8
B_RU = 12
B_MERGE = 20
B_OUT = 36
B_FFN = 40
FFN_IT = DFF // 256
B_DOWN = B_FFN + 2 * FFN_IT
DOWN_BLKS = KF // 2
N_BLKS = B_DOWN + DOWN_BLKS

K_QK, K_LR, K_R, K_U, K_GA, K_GB, K_BGK, K_GN, K_N1, K_N2, K_END = 0, 8, 9, 17, 25, 33, 41, 45, 47, 55, 63

KB = 1024
BASE = 16512


def build(nc, x, wstream, w_lr, cols, vbias, lnw, lnb, sgub, sgu_wt, w_gk2, ident_d, causal_d, finalw, out):
    with ExitStack() as ctx:
        def sb(name, kb, shape, dtype=F32):
            return nc.alloc_sbuf_tensor_at(name, shape, dtype, offset=BASE + int(kb * KB))

        def sem(name):
            return ctx.enter_context(nc.semaphore(name))

        raw = [sb(f"raw{s}", 8 * s, [P, BLK]) for s in range(2)]
        w_hi = [sb(f"w_hi{s}", 16 + 8 * s, [P, BLK], F32R) for s in range(2)]
        w_lo = [sb(f"w_lo{s}", 32 + 8 * s, [P, BLK], F32R) for s in range(2)]
        xt_hi = sb("xt_hi", 48, [P, KD, SEQ], F32R)
        xt_lo = sb("xt_lo", 64, [P, KD, SEQ], F32R)
        vgs = sb("vgs", 80, [P, 2, TT, D])
        ya_hi = sb("ya_hi", 80, [P, KD, SEQ], F32R)
        ya_lo = sb("ya_lo", 96, [P, KD, SEQ], F32R)
        h = sb("h", 80, [P, TT, D])
        hn = sb("hn", 96, [P, 2, D])
        fw = sb("fw", 108, [P, D])
        xn_in = sb("xn_in", 112, [P, TT, D])
        vbias_bc = sb("vbias_bc", 128, [P, 2, D])
        lnw_bc = sb("lnw_bc", 136, [P, D])
        lnb_bc = sb("lnb_bc", 140, [P, D])
        ya = sb("ya", 112, [P, KD, SEQ])
        yb = sb("yb", 128, [P, KD, SEQ])
        mg_hi = sb("mg_hi", 112, [P, KD, SEQ], F32R)
        mg_lo = sb("mg_lo", 128, [P, KD, SEQ], F32R)
        act = sb("act", 112, [P, KF, SEQ])
        qk = sb("qk", 144, [P, 2 * HEADS, SEQ])
        yb_hi = sb("yb_hi", 144, [P, KD, SEQ], F32R)
        yb_lo = sb("yb_lo", 160, [P, KD, SEQ], F32R)
        htmp = [sb(f"htmp{s}", 144 + 4 * s, [P, 2, 4, P]) for s in range(2)]
        xnat = sb("xnat", 160, [P, 2, D])
        xtmp = sb("xtmp", 168, [P, 2, 4, P])
        sq_junk0 = sb("sq_junk0", 172, [P, D])
        sq_junk = sb("sq_junk", 160, [P, D])
        sq_junk2 = sb("sq_junk2", 176, [P, D])
        g = sb("g", 160, [P, HEADS, SEQ])
        cum = sb("cum", 168, [P, NCH, CHUNK])
        rest = sb("rest", 170, [P, NCH, CHUNK])
        expb = sb("expb", 172, [P, NCH, CHUNK])
        ah = [sb(f"ah{s}", 160 + 4 * s, [P, 2, SEQ], F32R) for s in range(2)]
        al = [sb(f"al{s}", 168 + 4 * s, [P, 2, SEQ], F32R) for s in range(2)]
        ken = sb("ken", 176, [P, TT, P])
        osq = sb("osq", 176, [P, SEQ])
        sct = sb("sct", 178, [P, TT, P])
        vst = sb("vst", 180, [P, TT, DV])
        vns = sb("vns", 184, [P, TT, DV])
        state = sb("state", 188, [P, NCH - 1, DV])
        rs = sb("rs", 195, [P, SEQ])
        lr_raw = sb("lr_raw", 180, [P, KD, P])
        lr_hi = sb("lr_hi", 184, [P, KD, P], F32R)
        lr_lo = sb("lr_lo", 188, [P, KD, P], F32R)
        glr = sb("glr", 192, [P, SEQ])
        gk2 = sb("gk2", 195, [LOWRANK, HEADS * DK])
        zabs = sb("zabs", 180, [P, HEADS, SEQ])
        sg_a = sb("sg_a", 176, [P, 2, SEQ])
        sg_b = sb("sg_b", 180, [P, 2, SEQ])
        prod_a = sb("prod_a", 184, [P, 2, SEQ])
        prod_b = sb("prod_b", 188, [P, 2, SEQ])
        sil = sb("sil", 176, [P, 2, SEQ])
        sgub_bc = sb("sgub_bc", 197, [P, GROUPS, P])
        swt = sb("swt", 201, [P, GROUPS, P])
        ident = sb("ident", 205, [P, P])
        ones_dv = sb("ones_dv", 205.5, [P, P])
        keep = sb("keep", 206, [P, SEQ], BF16)
        causal = sb("causal", 207, [P, P], U8)
        par = sb("par", 207.125, [P, K_END])
        small = sb("small", 207.375, [P, 24])
        ms, sd, rstd = small[:, 0:4], small[:, 4:8], small[:, 8:12]
        eps = small[:, 12:13]
        scores_seen = sb("scores_seen", 207.5, [P, 1])
        warm = [small[:, 13 + n:14 + n] for n in range(3)]
        first_ms, second_sum = small[:, 16:20], small[:, 20:24]
        decay = small[:, 16:24]
        causal_f = sb("causal_f", 194.5, [P, P])
        bnst = sb("bnst", 194, [P, TT, 2, 6])
        bnag = sb("bnag", 194.25, [P, TT, 2])

        bank = [ctx.enter_context(nc.psum_tensor(f"bank{b}", [P, HALF], F32)) for b in range(8)]

        raw_landed = [sem(f"raw_landed{s}") for s in range(2)]
        first_half_low, second_half_low = sem("first_half_low"), sem("second_half_low")
        hi_ready, lo_ready, block_used = sem("hi_ready"), sem("lo_ready"), sem("block_used")
        x_landed = [sem(f"x_landed{t}") for t in range(TT)]
        h_landed, fw_landed, lr_landed = sem("h_landed"), sem("fw_landed"), sem("lr_landed")
        par_landed, ident_landed, gk2_landed = sem("par_landed"), sem("ident_landed"), sem("gk2_landed")
        vbias_landed, ln_landed = sem("vbias_landed"), sem("ln_landed")
        sgub_landed, swt_landed, causal_landed = sem("sgub_landed"), sem("swt_landed"), sem("causal_landed")
        eps_set, keep_set, ones_set, sct_zeroed = sem("eps_set"), sem("keep_set"), sem("ones_set"), sem("sct_zeroed")
        causal_set, seen = sem("causal_set"), sem("seen")
        swt_masked = sem("swt_masked")
        sq_sum, sd_ready, rstd_ready, norm_ready = sem("sq_sum"), sem("sd_ready"), sem("rstd_ready"), sem("norm_ready")
        turned, turned_w, xt_hi_ready, xt_ready = sem("turned"), sem("turned_w"), sem("xt_hi_ready"), sem("xt_ready")
        lr_hi_ready, lr_lo_ready, lr_done, glr_ready = sem("lr_hi_ready"), sem("lr_lo_ready"), sem("lr_done"), sem("glr_ready")
        acc_done, acc_free = sem("acc_done"), sem("acc_free")
        tile_done, tile_free = sem("tile_done"), sem("tile_free")
        z_done, zabs_ready, zexp_ready, zln_ready, zmin_ready, g_ready = (
            sem("z_done"), sem("zabs_ready"), sem("zexp_ready"), sem("zln_ready"), sem("zmin_ready"), sem("g_ready"))
        vgelu_ready, bn_ready, bnag_ready, vsd_ready, vrstd_ready, vnorm_ready, vscaled, vn_ready = (
            sem("vgelu_ready"), sem("bn_ready"), sem("bnag_ready"), sem("vsd_ready"), sem("vrstd_ready"),
            sem("vnorm_ready"), sem("vscaled"), sem("vn_ready"))
        cum_ready, rest_ready, exp_ready, decayed = sem("cum_ready"), sem("rest_ready"), sem("exp_ready"), sem("decayed")
        staged, kend_turned, ken_ready = sem("staged"), sem("kend_turned"), sem("ken_ready")
        scores_done, sct_ready, kv_done, state_ready = sem("scores_done"), sem("sct_ready"), sem("kv_done"), sem("state_ready")
        mixed_done, mixed_biased, ya_ready = sem("mixed_done"), sem("mixed_biased"), sem("ya_ready")
        o_done, sq_ready, osq_ready, ms_done, osd_ready, orstd_ready, yb_scaled, yb_ready = (
            sem("o_done"), sem("sq_ready"), sem("osq_ready"), sem("ms_done"), sem("osd_ready"),
            sem("orstd_ready"), sem("yb_scaled"), sem("yb_ready"))
        y_hi_ready = sem("y_hi_ready")
        branch_done, branch_free, prod_ready, msum_ready, mg_hi_ready = (
            sem("branch_done"), sem("branch_free"), sem("prod_ready"), sem("msum_ready"), sem("mg_hi_ready"))
        gate_done, up_done, sil_ready, act_ready = sem("gate_done"), sem("up_done"), sem("sil_ready"), sem("act_ready")
        ah_ready, al_ready = sem("ah_ready"), sem("al_ready")
        first_ms_ready = sem("first_ms_ready")
        y_ready, y_stored = sem("y_ready"), sem("y_stored")

        block = ctx.enter_context(nc.Block())

        def wk(t, s):
            return t[s][:, :].rearrange("p (k n) -> p k n", k=KD)

        def wn(t, s):
            return t[s][:, :].rearrange("p (k n) -> p k n", k=2)

        @block.sync
        def _(sp):
            sp.dma_start(xn_in[:, 0, :], x[0:P, :]).then_inc(x_landed[0], 16)
            sp.dma_start(ident[:, :], ident_d).then_inc(ident_landed, 16)
            sp.dma_start(par[:, :], cols).then_inc(par_landed, 16)
            sp.dma_start(raw[0][:, :], wstream[0]).then_inc(raw_landed[0], 16)
            for t in range(1, TT):
                sp.dma_start(xn_in[:, t, :], x[t * P:(t + 1) * P, :]).then_inc(x_landed[t], 16)
            sp.dma_start(raw[1][:, :], wstream[1]).then_inc(raw_landed[1], 16)
            sp.dma_start(vbias_bc[:, :, :].rearrange("p a n -> p (a n)"), vbias.partition_broadcast(P)).then_inc(vbias_landed, 16)
            sp.dma_start(lr_raw[:, :, :], w_lr).then_inc(lr_landed, 16)
            with sp.Fori(1, N_BLKS // 2) as i:
                for s in range(2):
                    sp.wait_ge(hi_ready, i * 2 + (s - 1))
                    sp.wait_ge(lo_ready, i * 2 + (s - 1))
                    sp.dma_start(raw[s][:, :], wstream[bass.ds(i * 2 + s, 1)].rearrange("a p n -> (a p) n")
                                 ).then_inc(raw_landed[s], 16)
            sp.wait_ge(hi_ready, N_BLKS - 2)
            sp.wait_ge(lo_ready, N_BLKS - 2)
            sp.dma_start(raw[0][:, :], wstream[N_BLKS - 1]).then_inc(raw_landed[0], 16)
            for t in range(TT - 1):
                sp.wait_ge(y_ready, 2 * t + 2)
                sp.dma_start(out[t * P:(t + 1) * P, :], h[:, t, :]).then_inc(y_stored, 16)
            for hf in range(2):
                sp.wait_ge(y_ready, 2 * TT - 1 + hf)
                hs = slice(hf * HALF, (hf + 1) * HALF)
                sp.dma_start(out[(TT - 1) * P:TT * P, hs], h[:, TT - 1, hs]).then_inc(y_stored, 16)
            sp.wait_ge(y_stored, 16 * (TT + 1))

        @block.gpsimd
        def _(pool):
            def low(b, s, landed):
                pool.wait_ge(raw_landed[s], landed)
                pool.wait_ge(hi_ready, b + 1)
                pool.tensor_tensor(w_lo[s][:, :], raw[s][:, :], w_hi[s][:, :], ALU.subtract).then_inc(lo_ready, 1)

            def low_shared(b, s, landed, n):
                pool.wait_ge(raw_landed[s], landed)
                pool.wait_ge(hi_ready, b + 1)
                pool.tensor_tensor(w_lo[s][:, 0:D], raw[s][:, 0:D], w_hi[s][:, 0:D], ALU.subtract
                                   ).then_inc(first_half_low, 1)
                pool.wait_ge(first_half_low, n)
                pool.wait_ge(second_half_low, n)
                pool.sem_inc(lo_ready, 1)

            low_shared(0, 0, 16, 1)
            low(1, 1, 16)
            pool.wait_ge(swt_landed, 16)
            pool.affine_select(out=swt[:, :, :], in_=swt[:, :, :], compare_op=ALU.is_ge, fill=0.0, base=0,
                               pattern=[[0, GROUPS], [1, P]], channel_multiplier=-1).then_inc(swt_masked, 1)
            with pool.Fori(1, B_FFN // 2 + 1) as i:
                for s in range(2):
                    low(i * 2 + s, s, i * 16 + 16)
            low_shared(B_FFN + 2, 0, 8 * (B_FFN + 4), 2)
            low(B_FFN + 3, 1, 8 * (B_FFN + 4))
            with pool.Fori(B_FFN // 2 + 2, N_BLKS // 2) as i:
                for s in range(2):
                    low(i * 2 + s, s, i * 16 + 16)
            low(N_BLKS - 1, 0, 16 * (N_BLKS // 2 + 1))

        @block.scalar
        def _(a):
            a.wait_ge(eps_set, 1)
            a.activation(warm[0], eps, ACT.Sqrt)

            def high(b, s, landed):
                a.wait_ge(raw_landed[s], landed)
                a.activation(w_hi[s][:, :], raw[s][:, :], ACT.Copy).then_inc(hi_ready, 1)

            def high2(b, s, used, n):
                a.wait_ge(used, n)
                high(b, s, (b - s) * 8 + 16)

            def stats(src, t, junk, n0):
                a.activation(junk[:, :], src, ACT.Square, accum_out=ms[:, t:t + 1]).then_inc(sq_sum, 1)
                a.wait_ge(sq_sum, n0 + t + 1)
                a.activation(sd[:, t:t + 1], ms[:, t:t + 1], ACT.Sqrt, bias=eps, scale=1.0 / D).then_inc(sd_ready, 1)

            def split_turned(tmp, t, n0):
                for hf in range(2):
                    a.wait_ge(turned_w, n0 + 2 * t + hf + 1)
                    a.activation(xt_hi[:, 4 * hf:4 * hf + 4, t * P:(t + 1) * P], tmp[:, hf], ACT.Copy
                                 ).then_inc(xt_hi_ready, 1)

            for t in range(TT):
                a.wait_ge(x_landed[t], 16)
                stats(xn_in[:, t, :], t, sq_junk0, 0)
                if t == 0:
                    a.dma_start(gk2[:, :], w_gk2).then_inc(gk2_landed, 16)
                    a.dma_start(causal_f[:, :], causal_d).then_inc(causal_landed, 16)
                    a.dma_start(swt[:, :, :], sgu_wt).then_inc(swt_landed, 16)
                    high(0, 0, 16)
                if t >= 1:
                    split_turned(xtmp, t - 1, 0)
                if t == 2:
                    high(1, 1, 16)
            split_turned(xtmp, TT - 1, 0)
            a.dma_start(lnw_bc[:, :], lnw.partition_broadcast(P)).then_inc(ln_landed, 16)
            a.dma_start(lnb_bc[:, :], lnb.partition_broadcast(P)).then_inc(ln_landed, 16)
            a.dma_start(sgub_bc[:, :, :].rearrange("p g t -> p (g t)"), sgub.partition_broadcast(P)).then_inc(sgub_landed, 16)
            a.wait_ge(lr_landed, 16)
            a.activation(lr_hi[:, :, :], lr_raw[:, :, :], ACT.Copy).then_inc(lr_hi_ready, 1)
            with a.Fori(0, 2) as i:
                for j in range(4):
                    if j < 3:
                        high2(i * 4 + (j + 2), j % 2, block_used, i * 3 + (j + 1))
                    else:
                        high2(i * 4 + (j + 2), j % 2, acc_done, i * 8 + 8)

            for t in range(TT):
                a.wait_ge(acc_free, 8 + 8 + 2 * t + 2)
                a.activation(vgs[:, 1, t, :], vgs[:, 1, t, :], ACT.Gelu_apprx_tanh).then_inc(vgelu_ready, 1)
            a.wait_ge(lr_done, 1)
            a.activation(glr[:, :], bank[4][:, :], ACT.Identity, bias=par[:, K_LR:K_LR + 1]).then_inc(glr_ready, 1)

            def queries_or_keys(i):
                for j in range(2):
                    for t in range(2):
                        n = 2 * j + t
                        a.wait_ge(tile_done, i * 4 + (n + 1))
                        a.activation(qk[:, i * 4 + n, :], bank[n][:, :], ACT.Identity,
                                     bias=par[:, i * 4 + (K_QK + n):i * 4 + (K_QK + n) + 1]).then_inc(tile_free, 1)
                    high2(i * 2 + (B_QK + 2 + j), j, tile_done, i * 4 + (2 * j + 2))

            queries_or_keys(0)
            for hd in range(HEADS):
                a.wait_ge(z_done, hd + 1)
                a.activation(zabs[:, hd, :], bank[4 + hd][:, :], ACT.Abs, bias=par[:, K_BGK + hd:K_BGK + hd + 1]
                             ).then_inc(zabs_ready, 1)
            a.wait_ge(zabs_ready, HEADS)
            a.activation(zabs[:, :, :], zabs[:, :, :], ACT.Exp, scale=-1.0).then_inc(zexp_ready, 1)
            a.wait_ge(zexp_ready, 1)
            a.activation(zabs[:, :, :], zabs[:, :, :], ACT.Ln, bias=1.0).then_inc(zln_ready, 1)
            a.wait_ge(bnag_ready, TT)
            a.activation(sd[:, :].unsqueeze(2), bnag[:, :, 1:2], ACT.Sqrt, bias=eps).then_inc(vsd_ready, 1)
            queries_or_keys(1)

            with a.Fori(0, HEADS) as i:
                def silu_r(t):
                    a.wait_ge(tile_done, i * 4 + (8 + t + 1))
                    a.activation(yb[:, bass.ds(i * 2 + t, 1), :], bank[t][:, :].unsqueeze(1), ACT.Silu,
                                 bias=par[:, bass.ds(i * 2 + (K_R + t), 1)]).then_inc(tile_free, 1)

                silu_r(0)
                a.wait_ge(cum_ready, i + 1)
                a.activation(expb[:, :, :], cum[:, :, :], ACT.Exp, scale=1.0 / GATE_NORM).then_inc(exp_ready, 1)
                a.wait_ge(rest_ready, i + 1)
                a.activation(rest[:, :, :], rest[:, :, :], ACT.Exp, scale=1.0 / GATE_NORM).then_inc(exp_ready, 1)
                a.activation(cum[:, :, :], cum[:, :, :], ACT.Exp, scale=-1.0 / GATE_NORM).then_inc(exp_ready, 1)
                a.wait_ge(vn_ready, 2 * TT)
                a.activation(vst[:, :, :], vgs[:, 0, :, bass.ds(i * DV, DV)], ACT.Copy).then_inc(staged, 1)
                a.activation(vns[:, :, :], vgs[:, 1, :, bass.ds(i * DV, DV)], ACT.Copy).then_inc(staged, 1)
                silu_r(1)
                high2(i * 2 + (B_RU + 2), 0, tile_done, i * 4 + 10)
                a.wait_ge(tile_done, i * 4 + 11)
                a.activation(ya[:, bass.ds(i * 2, 1), :], bank[0][:, :].unsqueeze(1), ACT.Gelu_apprx_tanh,
                             bias=par[:, bass.ds(i * 2 + K_U, 1)]).then_inc(tile_free, 1)
                a.wait_ge(kend_turned, i + 1)
                a.activation(ken[:, :, :], bank[4][:, :], ACT.Copy).then_inc(ken_ready, 1)
                a.wait_ge(tile_done, i * 4 + 12)
                a.activation(ya[:, bass.ds(i * 2 + 1, 1), :], bank[1][:, :].unsqueeze(1), ACT.Gelu_apprx_tanh,
                             bias=par[:, bass.ds(i * 2 + (K_U + 1), 1)]).then_inc(tile_free, 1)
                high2(i * 2 + (B_RU + 3), 1, tile_done, i * 4 + 12)
                a.wait_ge(o_done, i * 2 + 1)
                a.activation(osq[:, :], bank[6][:, :], ACT.Square).then_inc(sq_ready, 1)
                a.wait_ge(o_done, i * 2 + 2)
                a.activation(rs[:, :], bank[7][:, :], ACT.Square).then_inc(sq_ready, 1)
                a.wait_ge(ms_done, i + 1)
                a.activation(rs[:, :], bank[2][:, :], ACT.Sqrt, bias=eps).then_inc(osd_ready, 1)

            a.wait_ge(ya_ready, KD)
            for q in range(2):
                a.activation(ya_hi[:, 4 * q:4 * q + 4, :], ya[:, 4 * q:4 * q + 4, :], ACT.Copy).then_inc(y_hi_ready, 1)
            for q in range(2):
                a.wait_ge(yb_ready, 4 * q + 4)
                a.activation(yb_hi[:, 4 * q:4 * q + 4, :], yb[:, 4 * q:4 * q + 4, :], ACT.Copy).then_inc(y_hi_ready, 1)
            with a.Fori(0, KD // 2) as i:
                for j, (sg, kc) in enumerate(((sg_a, K_GA), (sg_b, K_GB))):
                    for t in range(2):
                        a.wait_ge(tile_done, i * 4 + (24 + 2 * j + t + 1))
                        a.activation(sg[:, t, :], bank[2 * j + t][:, :], ACT.Sigmoid,
                                     bias=par[:, bass.ds(i * 2 + (kc + t), 1)]).then_inc(tile_free, 1)
                    high2(i * 4 + (B_MERGE + 2 + j), j, tile_done, i * 4 + (24 + 2 * j + 2))
                high2(i * 4 + (B_MERGE + 4), 0, branch_done, i * 4 + 2)
                high2(i * 4 + (B_MERGE + 5), 1, branch_done, i * 4 + 4)
                for t in range(2):
                    a.wait_ge(msum_ready, i * 2 + (t + 1))
                    a.activation(mg_hi[:, bass.ds(i * 2 + t, 1), :], prod_a[:, t:t + 1, :], ACT.Copy
                                 ).then_inc(mg_hi_ready, 1)

            a.wait_ge(branch_done, 2 * KD)
            a.dma_start(h[:, :, :], x.rearrange("(t p) n -> p t n", p=P)).then_inc(h_landed, 16)
            a.dma_start(fw[:, :], finalw.partition_broadcast(P)).then_inc(fw_landed, 16)
            for j in range(3):
                high2(B_OUT + 2 + j, j % 2, block_used, 6 + j + 1)
            a.activation(warm[1], eps, ACT.Sqrt)

            def stats_h(t):
                a.wait_ge(acc_free, 24 + 2 * t + 2)
                stats(h[:, t, :], t, sq_junk, TT)

            def normalise_h(t):
                a.wait_ge(rstd_ready, TT + t + 1)
                if t >= 2:
                    a.wait_ge(turned, 2 * (TT + t - 1))
                a.activation(hn[:, t % 2, :], h[:, t, :], ACT.Identity, scale=rstd[:, t:t + 1]).then_inc(norm_ready, 1)

            stats_h(0)
            normalise_h(0)
            stats_h(1)
            normalise_h(1)
            split_turned(htmp[0], 0, 8)
            stats_h(2)
            split_turned(htmp[1], 1, 8)
            normalise_h(2)
            high2(B_FFN + 1, 1, acc_done, 24)
            stats_h(3)
            normalise_h(3)
            split_turned(htmp[0], 2, 8)
            split_turned(htmp[1], 3, 8)

            def gates(i, first=False):
                for t in range(2):
                    a.wait_ge(gate_done, i * 2 + (t + 1))
                    if not first:
                        a.wait_ge(act_ready, i * 2 + (t - 1))
                    a.activation(sil[:, t, :], bank[t][:, :], ACT.Silu).then_inc(sil_ready, 1)
                high2(i * 2 + (B_FFN + 2), 0, gate_done, i * 2 + 2)
                high2(i * 2 + (B_FFN + 3), 1, up_done, i * 2 + 2)

            def act_high(m, s):
                a.activation(ah[s][:, :, :], act[:, bass.ds(m * 2, 2), :], ACT.Copy).then_inc(ah_ready, 1)

            gates(0, True)
            a.wait_ge(act_ready, 2)
            act_high(0, 0)
            with a.Fori(1, FFN_IT) as i:
                gates(i)
            act_high(1, 1)
            high2(B_DOWN + 2, 0, block_used, 9 + 1)
            a.wait_ge(act_ready, KF)
            act_high(2, 0)
            with a.Fori(0, 4) as i:
                for s in range(2):
                    high2(i * 2 + (B_DOWN + 3 + s), 1 - s, block_used, i * 2 + (9 + 2 + s))
                    act_high(i * 2 + (3 + s), 1 - s)
            a.activation(warm[2], eps, ACT.Sqrt)
            for t in range(TT):
                a.wait_ge(acc_free, 32 + 2 * t + 1)
                a.activation(sq_junk2[:, 0:HALF], h[:, t, 0:HALF], ACT.Square, accum_out=ms[:, t:t + 1]).then_inc(sq_sum, 1)
                a.wait_ge(sq_sum, 2 * TT + 2 * t + 1)
                a.activation(first_ms[:, t:t + 1], ms[:, t:t + 1], ACT.Identity, bias=eps, scale=1.0 / D
                             ).then_inc(first_ms_ready, 1)
                a.wait_ge(acc_free, 32 + 2 * t + 2)
                a.activation(sq_junk2[:, HALF:D], h[:, t, HALF:D], ACT.Square, accum_out=second_sum[:, t:t + 1]).then_inc(sq_sum, 1)
                a.wait_ge(sq_sum, 2 * TT + 2 * t + 2)
                a.wait_ge(first_ms_ready, t + 1)
                a.activation(sd[:, t:t + 1], second_sum[:, t:t + 1], ACT.Sqrt, bias=first_ms[:, t:t + 1], scale=1.0 / D
                             ).then_inc(sd_ready, 1)

        @block.vector
        def _(v):
            v.memset(eps, EPS).then_inc(eps_set, 1)
            v.memset(keep[:, :], 1.0).then_inc(keep_set, 1)
            v.memset(ones_dv[:, :], 1.0 / DV).then_inc(ones_set, 1)
            v.memset(sct[:, :, :], 0.0).then_inc(sct_zeroed, 1)
            v.wait_ge(keep_set, 1)
            v.memset(keep[:, :].rearrange("p (c t) -> p c t", t=CHUNK)[:, :, 0:1], 0.0).then_inc(keep_set, 1)
            v.wait_ge(par_landed, 16)

            def normalise(dst, src, t, n0):
                v.wait_ge(sd_ready, n0 + t + 1)
                v.reciprocal(rstd[:, t:t + 1], sd[:, t:t + 1]).then_inc(rstd_ready, 1)
                v.wait_ge(rstd_ready, n0 + t + 1)
                if t >= 2:
                    v.wait_ge(turned, 2 * (n0 + t - 1))
                v.tensor_scalar(dst, src, rstd[:, t:t + 1], None, ALU.mult).then_inc(norm_ready, 1)

            def weigh_turned(tmp, t, n0, kw, depth):
                for hf in range(2):
                    n = n0 + 2 * t + hf
                    v.wait_ge(turned, n + 1)
                    if n - n0 >= depth:
                        v.wait_ge(xt_ready, n + 1 - depth)
                    w = par[:, kw + 4 * hf:kw + 4 * hf + 4].unsqueeze(2).broadcast_to([P, 4, P])
                    v.tensor_tensor(tmp[:, hf], bank[2 * t + hf][:, :].rearrange("p (k t) -> p k t", k=4), w, ALU.mult
                                    ).then_inc(turned_w, 1)

            def low_turned(tmp, t, n0):
                for hf in range(2):
                    n = n0 + 2 * t + hf
                    v.wait_ge(xt_hi_ready, n + 1)
                    v.tensor_tensor(xt_lo[:, 4 * hf:4 * hf + 4, t * P:(t + 1) * P], tmp[:, hf],
                                    xt_hi[:, 4 * hf:4 * hf + 4, t * P:(t + 1) * P], ALU.subtract).then_inc(xt_ready, 1)

            def low_second_half(b, s, landed):
                v.wait_ge(raw_landed[s], landed)
                v.wait_ge(hi_ready, b + 1)
                v.tensor_tensor(w_lo[s][:, D:BLK], raw[s][:, D:BLK], w_hi[s][:, D:BLK], ALU.subtract
                                ).then_inc(second_half_low, 1)

            normalise(xnat[:, 0, :], xn_in[:, 0, :], 0, 0)
            weigh_turned(xtmp, 0, 0, K_N1, 2)
            low_second_half(0, 0, 16)
            for t in range(1, TT):
                normalise(xnat[:, t % 2, :], xn_in[:, t, :], t, 0)
                if t >= 2:
                    weigh_turned(xtmp, t - 1, 0, K_N1, 2)
                low_turned(xtmp, t - 1, 0)
            weigh_turned(xtmp, TT - 1, 0, K_N1, 2)
            low_turned(xtmp, TT - 1, 0)
            v.wait_ge(lr_hi_ready, 1)
            v.tensor_tensor(lr_lo[:, :, :], lr_raw[:, :, :], lr_hi[:, :, :], ALU.subtract).then_inc(lr_lo_ready, 1)

            v.wait_ge(causal_landed, 16)
            v.tensor_copy(causal[:, :], causal_f[:, :]).then_inc(causal_set, 1)
            v.wait_ge(vbias_landed, 16)
            with v.Fori(0, 2) as i:
                for t in range(TT):
                    for hf in range(2):
                        v.wait_ge(acc_done, i * 8 + (2 * t + hf + 1))
                        cs = slice(hf * HALF, (hf + 1) * HALF)
                        v.tensor_tensor(vgs[:, bass.ds(i, 1), t, cs], bank[2 * t + hf][:, :].unsqueeze(1),
                                        vbias_bc[:, bass.ds(i, 1), cs], ALU.add).then_inc(acc_free, 1)

            for t in range(TT):
                v.wait_ge(vgelu_ready, t + 1)
                for hf in range(2):
                    v.bn_stats(bnst[:, t, hf, :], vgs[:, 1, t, hf * HALF:(hf + 1) * HALF]).then_inc(bn_ready, 1)
                v.wait_ge(bn_ready, 2 * t + 2)
                v.bn_aggr(bnag[:, t, :], bnst[:, t, :, :]).then_inc(bnag_ready, 1)
            for hd in range(HEADS):
                v.wait_ge(zabs_ready, hd + 1)
                v.tensor_scalar(g[:, hd, :], bank[4 + hd][:, :], par[:, K_BGK + hd:K_BGK + hd + 1], 0.0,
                                ALU.add, ALU.min).then_inc(zmin_ready, 1)
            v.wait_ge(zln_ready, 1)
            v.wait_ge(zmin_ready, HEADS)
            v.tensor_tensor(g[:, :, :], g[:, :, :], zabs[:, :, :], ALU.subtract).then_inc(g_ready, 1)
            v.wait_ge(vsd_ready, 1)
            v.reciprocal(rstd[:, :], sd[:, :]).then_inc(vrstd_ready, 1)
            v.wait_ge(vrstd_ready, 1)
            v.wait_ge(ln_landed, 32)
            for t in range(TT):
                v.tensor_scalar(vgs[:, 1, t, :], vgs[:, 1, t, :], bnag[:, t, 0:1], rstd[:, t:t + 1],
                                ALU.subtract, ALU.mult).then_inc(vnorm_ready, 1)
            for t in range(TT):
                v.wait_ge(vnorm_ready, t + 1)
                v.tensor_tensor(vgs[:, 1, t, :], vgs[:, 1, t, :], lnw_bc[:, :], ALU.mult).then_inc(vscaled, 1)
            for t in range(TT):
                v.wait_ge(vscaled, t + 1)
                v.tensor_tensor(vgs[:, 1, t, :], vgs[:, 1, t, :], lnb_bc[:, :], ALU.add).then_inc(vn_ready, 2)

            v.wait_ge(g_ready, 1)
            v.wait_ge(keep_set, 2)
            v.wait_ge(sct_zeroed, 1)
            v.wait_ge(sgub_landed, 16)
            v.wait_ge(causal_set, 1)
            with v.Fori(0, HEADS) as i:
                v.tensor_tensor_scan(cum[:, :, :].rearrange("p c t -> p (c t)"), keep[:, :],
                                     g[:, bass.ds(i, 1), :].rearrange("p a t -> p (a t)"), 0.0,
                                     ALU.mult, ALU.add).then_inc(cum_ready, 1)
                v.wait_ge(cum_ready, i + 1)
                v.tensor_tensor(rest[:, :, :], cum[:, :, CHUNK - 1:CHUNK].broadcast_to([P, NCH, CHUNK]), cum[:, :, :],
                                ALU.subtract).then_inc(rest_ready, 1)
                v.wait_ge(exp_ready, i * 3 + 1)
                v.wait_ge(tile_free, 4 + 8)
                v.tensor_copy(decay.unsqueeze(2), expb[:, :, CHUNK - 1:CHUNK]).then_inc(decayed, 1)
                v.wait_ge(decayed, i * 4 + 1)
                v.scalar_tensor_tensor(expb[:, :, :].rearrange("p c t -> p (c t)"),
                                       qk[:, bass.ds(i, 1), :].rearrange("p a t -> p (a t)"), DK ** -0.5,
                                       expb[:, :, :].rearrange("p c t -> p (c t)"), ALU.mult, ALU.mult).then_inc(decayed, 1)
                v.wait_ge(exp_ready, i * 3 + 2)
                kh = qk[:, bass.ds(i + HEADS, 1), :].rearrange("p a (c t) -> p (a c) t", t=CHUNK)
                v.tensor_tensor(rest[:, :, :], kh, rest[:, :, :], ALU.mult).then_inc(decayed, 1)
                v.wait_ge(exp_ready, i * 3 + 3)
                v.tensor_tensor(cum[:, :, :], kh, cum[:, :, :], ALU.mult).then_inc(decayed, 1)

                v.wait_ge(scores_done, i + 1)
                v.memset(scores_seen[:, :], 0.0).then_inc(seen, 1)
                v.copy_predicated(sct[:, :, :], causal[:, :].unsqueeze(1).broadcast_to([P, TT, P]),
                                  bank[5][:, :].rearrange("p (t s) -> p t s", t=TT)).then_inc(sct_ready, 1)

                for n in range(NCH - 1):
                    if n % 2 == 0:
                        v.wait_ge(kv_done, i * 4 + (n // 2 + 1))
                    kv = bank[KV_BANKS[n % 4]][:, 0:DV]
                    if n == 0:
                        v.tensor_copy(state[:, 0, :], kv).then_inc(state_ready, 1)
                    else:
                        v.wait_ge(state_ready, i * 7 + n)
                        v.scalar_tensor_tensor(state[:, n, :], state[:, n - 1, :], decay[:, n:n + 1], kv,
                                               ALU.mult, ALU.add).then_inc(state_ready, 1)

                def gate_mixed(q):
                    v.wait_ge(mixed_done, i * 2 + (q + 1))
                    m = bank[4 - q][:, :].rearrange("p (n t) -> p n t", n=TT)
                    v.tensor_tensor(m, m, sgub_bc[:, bass.ds(i * 2 + q, 1), :].broadcast_to([P, TT, P]), ALU.add
                                    ).then_inc(mixed_biased, 1)
                    v.wait_ge(mixed_biased, i * 2 + (q + 1))
                    v.wait_ge(tile_free, i * 4 + (4 + 8 + 3 + q))
                    yg = ya[:, bass.ds(i * 2 + q, 1), :].rearrange("p a t -> p (a t)")
                    v.tensor_tensor(yg, yg, bank[4 - q][:, :], ALU.mult).then_inc(ya_ready, 1)

                v.wait_ge(sq_ready, i * 2 + 2)
                v.tensor_tensor(osq[:, :], osq[:, :], rs[:, :], ALU.add).then_inc(osq_ready, 1)
                gate_mixed(0)
                gate_mixed(1)
                for q in range(2):
                    yh = yb[:, bass.ds(i * 2 + q, 1), :].rearrange("p a t -> p (a t)")
                    v.scalar_tensor_tensor(yh, bank[6 + q][:, :], par[:, K_GN + q:K_GN + q + 1], yh, ALU.mult, ALU.mult
                                           ).then_inc(yb_scaled, 1)
                v.wait_ge(osd_ready, i + 1)
                v.reciprocal(rs[:, :], rs[:, :]).then_inc(orstd_ready, 1)
                v.wait_ge(orstd_ready, i + 1)
                v.wait_ge(yb_scaled, i * 2 + 2)
                for q in range(2):
                    yh = yb[:, bass.ds(i * 2 + q, 1), :].rearrange("p a t -> p (a t)")
                    v.tensor_tensor(yh, yh, rs[:, :], ALU.mult).then_inc(yb_ready, 1)

            for q in range(2):
                ks = slice(4 * q, 4 * q + 4)
                v.wait_ge(y_hi_ready, q + 1)
                v.tensor_tensor(ya_lo[:, ks, :], ya[:, ks, :], ya_hi[:, ks, :], ALU.subtract)
            v.wait_ge(y_hi_ready, 3)
            v.tensor_tensor(yb_lo[:, 0:4, :], yb[:, 0:4, :], yb_hi[:, 0:4, :], ALU.subtract)
            v.wait_ge(y_hi_ready, 4)
            v.tensor_tensor(yb_lo[:, 4:8, :], yb[:, 4:8, :], yb_hi[:, 4:8, :], ALU.subtract).then_inc(branch_free, 1)

            with v.Fori(0, KD // 2) as i:
                v.wait_ge(tile_free, i * 4 + (4 + 24 + 4))
                for q in range(2):
                    v.wait_ge(branch_done, i * 4 + (q + 1))
                    v.tensor_tensor(prod_a[:, q, :], bank[4 + q][:, :], sg_a[:, q, :], ALU.mult).then_inc(prod_ready, 1)
                for q in range(2):
                    v.wait_ge(branch_done, i * 4 + (q + 3))
                    v.tensor_tensor(prod_b[:, q, :], bank[6 + q][:, :], sg_b[:, q, :], ALU.mult).then_inc(prod_ready, 1)
                for q in range(2):
                    v.wait_ge(prod_ready, i * 4 + (q + 3))
                    v.tensor_tensor(prod_a[:, q, :], prod_a[:, q, :], prod_b[:, q, :], ALU.add).then_inc(msum_ready, 1)
                for q in range(2):
                    v.wait_ge(mg_hi_ready, i * 2 + (q + 1))
                    v.tensor_tensor(mg_lo[:, bass.ds(i * 2 + q, 1), :], prod_a[:, q:q + 1, :],
                                    mg_hi[:, bass.ds(i * 2 + q, 1), :], ALU.subtract).then_inc(branch_free, 1)

            def residual(t, n0):
                for hf in range(2):
                    v.wait_ge(acc_done, n0 + 2 * t + hf + 1)
                    hs = h[:, t, hf * HALF:(hf + 1) * HALF]
                    v.tensor_tensor(hs, bank[2 * t + hf][:, :], hs, ALU.add).then_inc(acc_free, 1)

            v.wait_ge(h_landed, 16)

            def rstd_h(t):
                v.wait_ge(sd_ready, TT + t + 1)
                v.reciprocal(rstd[:, t:t + 1], sd[:, t:t + 1]).then_inc(rstd_ready, 1)

            residual(0, 16)
            rstd_h(0)
            residual(1, 16)
            rstd_h(1)
            weigh_turned(htmp[0], 0, 8, K_N2, 4)
            residual(2, 16)
            low_turned(htmp[0], 0, 8)
            weigh_turned(htmp[1], 1, 8, K_N2, 4)
            rstd_h(2)
            low_turned(htmp[1], 1, 8)
            residual(3, 16)
            rstd_h(3)
            weigh_turned(htmp[0], 2, 8, K_N2, 4)
            low_turned(htmp[0], 2, 8)
            weigh_turned(htmp[1], 3, 8, K_N2, 4)
            low_turned(htmp[1], 3, 8)

            def gated(i):
                for t in range(2):
                    v.wait_ge(sil_ready, i * 2 + (t + 1))
                    v.wait_ge(up_done, i * 2 + (t + 1))
                    v.tensor_tensor(act[:, bass.ds(i * 2 + t, 1), :], bank[2 + t][:, :].unsqueeze(1),
                                    sil[:, t:t + 1, :], ALU.mult).then_inc(act_ready, 1)

            def act_low(m, s):
                v.wait_ge(ah_ready, m + 1)
                v.tensor_tensor(al[s][:, :, :], act[:, bass.ds(m * 2, 2), :], ah[s][:, :, :], ALU.subtract
                                ).then_inc(al_ready, 1)

            low_second_half(B_FFN + 2, 0, 8 * (B_FFN + 4))
            gated(0)
            act_low(0, 0)
            with v.Fori(1, FFN_IT) as i:
                gated(i)
            act_low(1, 1)
            act_low(2, 0)
            with v.Fori(0, 4) as i:
                for s in range(2):
                    act_low(i * 2 + (3 + s), 1 - s)
            v.wait_ge(fw_landed, 16)

            def finish(t):
                v.wait_ge(sd_ready, 2 * TT + t + 1)
                v.reciprocal(rstd[:, t:t + 1], sd[:, t:t + 1]).then_inc(rstd_ready, 1)
                v.wait_ge(rstd_ready, 2 * TT + t + 1)
                for hf in range(2):
                    hs = slice(hf * HALF, (hf + 1) * HALF)
                    v.scalar_tensor_tensor(h[:, t, hs], h[:, t, hs], rstd[:, t:t + 1], fw[:, hs], ALU.mult, ALU.mult
                                           ).then_inc(y_ready, 1)

            residual(0, 24)
            finish(0)
            residual(1, 24)
            residual(2, 24)
            finish(1)
            residual(3, 24)
            finish(2)
            finish(3)

        @block.tensor
        def _(pe):
            def turn(src, dst0, t, n0):
                pe.wait_ge(norm_ready, n0 + t + 1)
                for hf in range(2):
                    for k in range(4):
                        c = (4 * hf + k) * P
                        last = pe.transpose(bank[dst0 + hf][:, k * P:(k + 1) * P], src[:, c:c + P], ident[:, :])
                    last.then_inc(turned, 1)

            def arrived(b):
                pe.wait_ge(hi_ready, b + 1)
                pe.wait_ge(lo_ready, b + 1)

            def tile_T(dst, wh, wl, t, rh, rl, ts=slice(0, SEQ)):
                cs = slice(t * P, (t + 1) * P)
                for k in range(KD):
                    pe.matmul(dst, wh[:, k, cs], rh[:, k, ts], start=(k == 0), stop=False)
                    pe.matmul(dst, wh[:, k, cs], rl[:, k, ts], start=False, stop=False)
                    last = pe.matmul(dst, wl[:, k, cs], rh[:, k, ts], start=False, stop=(k == KD - 1))
                return last

            def block_N(s, lh, ll, first, last, before=None, after=None, between=None):
                wh, wl = wn(w_hi, s), wn(w_lo, s)
                for t in range(TT):
                    if before is not None:
                        before(t)
                    for hf in range(2):
                        cs = slice(hf * HALF, (hf + 1) * HALF)
                        for k in range(2):
                            ts = slice(t * P, (t + 1) * P)
                            dst = bank[2 * t + hf][:, :]
                            pe.matmul(dst, lh[:, k, ts], wh[:, k, cs], start=(first and k == 0), stop=False)
                            pe.matmul(dst, lh[:, k, ts], wl[:, k, cs], start=False, stop=False)
                            mm = pe.matmul(dst, ll[:, k, ts], wh[:, k, cs], start=False, stop=(last and k == 1))
                        if last:
                            mm.then_inc(acc_done, 1)
                        if between is not None and hf == 0:
                            between(t)
                    if after is not None:
                        after(t)
                if not last:
                    mm.then_inc(block_used, 1)

            pe.wait_ge(ident_landed, 16)
            pe.sem_inc(acc_free, 8)
            turn(xnat[:, 0, :], 0, 0, 0)
            turn(xnat[:, 1, :], 2, 1, 0)
            arrived(0)

            def turned_x(t):
                pe.wait_ge(xt_ready, 2 * t + 2)

            def turn_x(t):
                if t + 2 < TT:
                    turn(xnat[:, t % 2, :], 2 * (t + 2), t + 2, 0)
            block_N(0, xt_hi[:, 0:2, :], xt_lo[:, 0:2, :], True, False, turned_x, turn_x)
            for b in range(1, B_QK):
                i, j = b // 4, b % 4
                arrived(b)

                def free(t):
                    if b == 4:
                        pe.wait_ge(acc_free, 8 + 2 * t + 2)
                ks = slice(2 * j, 2 * j + 2)
                block_N(j % 2, xt_hi[:, ks, :], xt_lo[:, ks, :], j == 0, j == 3, free)

            pe.wait_ge(lr_lo_ready, 1)
            pe.wait_ge(acc_free, 8 + 8 + 5)
            tile_T(bank[4][:, :], lr_hi, lr_lo, 0, xt_hi, xt_lo).then_inc(lr_done, 1)

            def queries_or_keys(i):
                for j in range(2):
                    arrived(i * 2 + (B_QK + j))
                    for t in range(2):
                        n = 2 * j + t
                        pe.wait_ge(tile_free, i * 4 + (n + 1))
                        tile_T(bank[n][:, :], wk(w_hi, j), wk(w_lo, j), t, xt_hi, xt_lo).then_inc(tile_done, 1)

            pe.wait_ge(acc_free, 8 + 16)
            pe.sem_inc(tile_free, 4)
            queries_or_keys(0)
            pe.wait_ge(gk2_landed, 16)
            pe.wait_ge(glr_ready, 1)
            for hd in range(HEADS):
                pe.matmul(bank[4 + hd][:, :], gk2[:, hd * DK:(hd + 1) * DK], glr[0:LOWRANK, :], start=True, stop=True
                          ).then_inc(z_done, 1)
            queries_or_keys(1)

            pe.wait_ge(ones_set, 1)
            pe.wait_ge(swt_masked, 1)
            with pe.Fori(0, HEADS) as i:
                def gate_tile(j, t):
                    n = 2 * j + t
                    pe.wait_ge(tile_free, i * 4 + (8 + n + 3))
                    tile_T(bank[t][:, :], wk(w_hi, j), wk(w_lo, j), t, xt_hi, xt_lo).then_inc(tile_done, 1)

                def mix(q):
                    w = swt[:, bass.ds(i * 2 + q, 1), :].rearrange("p a t -> p (a t)")
                    for n in range(TT):
                        mm = pe.matmul(bank[4 - q][:, n * P:(n + 1) * P], vns[:, n, q * P:(q + 1) * P], w,
                                       start=True, stop=True)
                    mm.then_inc(mixed_done, 1)

                arrived(i * 2 + B_RU)
                gate_tile(0, 0)
                gate_tile(0, 1)
                arrived(i * 2 + (B_RU + 1))
                gate_tile(1, 0)
                pe.wait_ge(decayed, i * 4 + 4)
                for t in range(TT):
                    mm = pe.transpose(bank[4][:, t * P:(t + 1) * P], rest[:, 2 * t:2 * t + 2, :].rearrange("p c t -> p (c t)"),
                                      ident[:, :])
                mm.then_inc(kend_turned, 1)
                for t in range(TT):
                    mm = pe.matmul(bank[5][:, t * P:(t + 1) * P], cum[:, 2 * t:2 * t + 2, :].rearrange("p c t -> p (c t)"),
                                   expb[:, 2 * t:2 * t + 2, :].rearrange("p c t -> p (c t)"), start=True, stop=True)
                mm.then_inc(scores_done, 1)
                gate_tile(1, 1)
                pe.wait_ge(ken_ready, i + 1)
                pe.wait_ge(staged, i * 2 + 2)
                pe.wait_ge(sct_ready, i + 1)
                for n in range(NCH - 1):
                    if n in (4, 6):
                        pe.wait_ge(state_ready, i * 7 + (n - 2))
                    r0 = (n % 2) * CHUNK
                    mm = pe.matmul(bank[KV_BANKS[n % 4]][:, 0:DV],
                                   ken[r0:r0 + CHUNK, n // 2, :], vst[r0:r0 + CHUNK, n // 2, :], start=True, stop=True)
                    if n % 2 == 1 or n == NCH - 2:
                        mm.then_inc(kv_done, 1)
                for q in range(2):
                    qs = slice(q * P, (q + 1) * P)
                    for t in range(TT):
                        pe.matmul(bank[6 + q][:, t * P:(t + 1) * P], vst[:, t, qs], sct[:, t, :],
                                  start=(t == 0), stop=(t == 0), skip_group_check=True)
                        for n in (2 * t, 2 * t + 1):
                            if n > 0:
                                if q == 0:
                                    pe.wait_ge(state_ready, i * 7 + n)
                                mm = pe.matmul(bank[6 + q][:, n * CHUNK:(n + 1) * CHUNK], state[:, n - 1, qs], expb[:, n, :],
                                               start=False, stop=True, skip_group_check=True)
                    mm.then_inc(o_done, 1)
                mix(0)
                mix(1)
                pe.wait_ge(osq_ready, i + 1)
                pe.matmul(bank[2][:, :], ones_dv[:, :], osq[:, :], start=True, stop=True).then_inc(ms_done, 1)

            pe.wait_ge(tile_free, 4 + 24)
            with pe.Fori(0, KD // 2) as i:
                for j in range(2):
                    arrived(i * 4 + (B_MERGE + j))
                    for t in range(2):
                        n = 2 * j + t
                        pe.wait_ge(tile_free, i * 4 + (24 + n + 1))
                        if n == 2:
                            pe.wait_ge(osd_ready, HEADS)
                        if n == 3:
                            pe.wait_ge(ya_ready, KD)
                        tile_T(bank[n][:, :], wk(w_hi, j), wk(w_lo, j), t, xt_hi, xt_lo).then_inc(tile_done, 1)
                pe.wait_ge(branch_free, i * 2 + 1)
                for j, (yh, yl) in enumerate(((ya_hi, ya_lo), (yb_hi, yb_lo))):
                    arrived(i * 4 + (B_MERGE + 2 + j))
                    for t in range(2):
                        tile_T(bank[4 + 2 * j + t][:, :], wk(w_hi, j), wk(w_lo, j), t, yh, yl).then_inc(branch_done, 1)

            pe.wait_ge(tile_free, 4 + 40)
            for j in range(4):
                arrived(B_OUT + j)
                pe.wait_ge(branch_free, 2 * j + 3)
                ks = slice(2 * j, 2 * j + 2)

                def products_read(t):
                    if j == 0 and t >= 2:
                        pe.wait_ge(prod_ready, 2 * KD - 2 + 2 * (t - 2))

                def turn_h(t):
                    if j == 3 and t >= 2:
                        turn(hn[:, t - 2, :], 2 * (t - 2), t - 2, TT)
                block_N(j % 2, mg_hi[:, ks, :], mg_lo[:, ks, :], j == 0, j == 3, products_read, None, turn_h)

            s0, s1 = slice(0, SEQ // 2), slice(SEQ // 2, SEQ)
            arrived(B_FFN)
            pe.wait_ge(xt_ready, 8 + 4)
            for t in range(2):
                tile_T(bank[t][:, s0], wk(w_hi, 0), wk(w_lo, 0), t, xt_hi, xt_lo, s0)
                turn(hn[:, t, :], 4 + 2 * t, 2 + t, TT)
            arrived(B_FFN + 1)
            for t in range(2):
                tile_T(bank[2 + t][:, s0], wk(w_hi, 1), wk(w_lo, 1), t, xt_hi, xt_lo, s0)
            pe.wait_ge(xt_ready, 16)
            for t in range(2):
                tile_T(bank[t][:, s1], wk(w_hi, 0), wk(w_lo, 0), t, xt_hi, xt_lo, s1).then_inc(gate_done, 1)
            for t in range(2):
                tile_T(bank[2 + t][:, s1], wk(w_hi, 1), wk(w_lo, 1), t, xt_hi, xt_lo, s1).then_inc(up_done, 1)
            with pe.Fori(1, FFN_IT) as i:
                arrived(i * 2 + B_FFN)
                for t in range(2):
                    pe.wait_ge(sil_ready, i * 2 + (t - 1))
                    tile_T(bank[t][:, :], wk(w_hi, 0), wk(w_lo, 0), t, xt_hi, xt_lo).then_inc(gate_done, 1)
                arrived(i * 2 + (B_FFN + 1))
                for t in range(2):
                    pe.wait_ge(act_ready, i * 2 + (t - 1))
                    tile_T(bank[2 + t][:, :], wk(w_hi, 1), wk(w_lo, 1), t, xt_hi, xt_lo).then_inc(up_done, 1)

            def down(m, s, first=False, last=False):
                arrived(m + B_DOWN)
                pe.wait_ge(al_ready, m + 1)

                def free(t):
                    if first and t == 0:
                        pe.wait_ge(sil_ready, KF)
                    if first and t == 1:
                        pe.wait_ge(act_ready, KF)
                block_N(s, ah[s], al[s], first, last, free)

            down(0, 0, first=True)
            with pe.Fori(0, 4) as i:
                down(i * 2 + 1, 1)
                down(i * 2 + 2, 0)
            down(DOWN_BLKS - 2, 1)
            down(DOWN_BLKS - 1, 0, last=True)


def _t_block(w, c0):
    return w[:, c0:c0 + 256].reshape(KD, P, 256).transpose(1, 0, 2).reshape(P, BLK)


def _n_block(w, j, c0=0):
    return w[256 * j:256 * (j + 1), c0:c0 + D].reshape(2, P, D).transpose(1, 0, 2).reshape(P, BLK)


def _tiles(v):
    return v.reshape(-1, P).T


def kernel(x, norm1_w, w_in, b_in, sgu_ln_w, sgu_ln_b, sgu_w, sgu_b, w_gk2, b_gk, gla_norm_w,
           w_branch_a, w_branch_b, w_out, norm2_w, w_ffn_gate, w_ffn_up, w_ffn_down, final_norm_w):
    import concourse.bacc as bacc
    from concourse.bass_utils import run_bass_kernel_spmd

    f = np.asarray
    x2, wi, bi = f(x)[0], f(w_in)[0], f(b_in)[0]
    wa, wb, wo = f(w_branch_a)[0], f(w_branch_b)[0], f(w_out)[0]
    wg, wu, wd = f(w_ffn_gate)[0], f(w_ffn_up)[0], f(w_ffn_down)[0]

    blocks = [_n_block(wi, j, C_VG) for j in range(4)] + [_n_block(wi, j, C_V) for j in range(4)]
    blocks += [_t_block(wi, C_Q + 256 * j) for j in range(4)]
    for i in range(4):
        blocks += [_t_block(wi, C_R + 256 * i), _t_block(wi, C_U + 256 * i)]
    for i in range(4):
        blocks += [_t_block(wi, C_GA + 256 * i), _t_block(wi, C_GB + 256 * i),
                   _t_block(wa, 256 * i), _t_block(wb, 256 * i)]
    blocks += [_n_block(wo, j) for j in range(4)]
    for i in range(FFN_IT):
        blocks += [_t_block(wg, 256 * i), _t_block(wu, 256 * i)]
    blocks += [_n_block(wd, j) for j in range(DOWN_BLKS)]

    cols = np.concatenate([
        _tiles(bi[C_Q:C_Q + D]), _tiles(bi[C_LR:C_LR + P]), _tiles(bi[C_R:C_R + D]), _tiles(bi[C_U:C_U + D]),
        _tiles(bi[C_GA:C_GA + D]), _tiles(bi[C_GB:C_GB + D]), _tiles(f(b_gk)[0]), _tiles(f(gla_norm_w)[0]),
        _tiles(f(norm1_w)[0]), _tiles(f(norm2_w)[0])], axis=1)
    tok = np.arange(P)
    causal = ((tok[:, None] <= tok[None, :]) & (tok[:, None] // CHUNK == tok[None, :] // CHUNK)).astype(np.float32)

    arrays = {
        "x": x2,
        "wstream": np.stack(blocks),
        "w_lr": wi[:, C_LR:C_LR + P].reshape(KD, P, P).transpose(1, 0, 2),
        "cols": cols,
        "vbias": np.concatenate([bi[C_VG:C_VG + D], bi[C_V:C_V + D]]),
        "lnw": f(sgu_ln_w)[0], "lnb": f(sgu_ln_b)[0],
        "sgub": f(sgu_b)[0].reshape(-1),
        "sgu_wt": f(sgu_w)[0].transpose(2, 0, 1),
        "w_gk2": f(w_gk2)[0],
        "ident_d": np.eye(P, dtype=np.float32),
        "causal_d": causal,
        "finalw": f(final_norm_w),
    }
    nc = bacc.Bacc("TRN2", target_bir_lowering=False, num_devices=1)
    arrays = {k: np.ascontiguousarray(a) for k, a in arrays.items()}
    aps = {k: nc.dram_tensor(k, a.shape, mybir.dt.from_np(a.dtype), kind="ExternalInput").ap() for k, a in arrays.items()}
    aps["out"] = nc.dram_tensor("out", (SEQ, D), F32, kind="ExternalOutput").ap()
    build(nc, **aps)
    r = run_bass_kernel_spmd(nc, [arrays], core_ids=[0])
    return r.results[0]["out"].reshape(1, SEQ, D)
```

```python
from contextlib import ExitStack

import numpy as np

import concourse.bass as bass
from concourse import mybir

ALU = mybir.AluOpType
ACT = mybir.ActivationFunctionType
F32 = mybir.dt.float32
F32R = mybir.dt.float32r
BF16 = mybir.dt.bfloat16
U8 = mybir.dt.uint8

P = 128
SEQ = 512
D = 1024
TT = SEQ // P
KD = D // P
HEADS = 4
DK = 128
DV = 256
CHUNK = 64
NCH = SEQ // CHUNK
GROUPS = 8
LOWRANK = 16
DFF = 2816
KF = DFF // P
EPS = 1e-6
GATE_NORM = 16.0
KV_BANKS = (2, 3, 4, 5)
BLK = 2048
HALF = 512

C_U, C_V, C_Q, C_K, C_VG, C_R, C_LR, C_GA, C_GB = 0, 1024, 2048, 2560, 3072, 4096, 5120, 5136, 6160

B_VG = 0
B_QK = 8
B_RU = 12
B_MERGE = 20
B_OUT = 36
B_FFN = 40
FFN_IT = DFF // 256
B_DOWN = B_FFN + 2 * FFN_IT
DOWN_BLKS = KF // 2
N_BLKS = B_DOWN + DOWN_BLKS

K_QK, K_LR, K_R, K_U, K_GA, K_GB, K_BGK, K_GN, K_N1, K_N2, K_END = 0, 8, 9, 17, 25, 33, 41, 45, 47, 55, 63

WARM_UP = 17
KB = 1024
BASE = 16512


def build(nc, x, x_t, wstream, w_lr, cols, vbias, lnw, lnb, sgub, sgu_wt, w_gk2, ident_d, causal_d, finalw, out):
    with ExitStack() as ctx:
        def sb(name, kb, shape, dtype=F32):
            return nc.alloc_sbuf_tensor_at(name, shape, dtype, offset=BASE + int(kb * KB))

        def sem(name):
            return ctx.enter_context(nc.semaphore(name))

        raw = [sb(f"raw{s}", 8 * s, [P, BLK]) for s in range(2)]
        w_hi = [sb(f"w_hi{s}", 16 + 8 * s, [P, BLK], F32R) for s in range(2)]
        w_lo = [sb(f"w_lo{s}", 32 + 8 * s, [P, BLK], F32R) for s in range(2)]
        xt_hi = sb("xt_hi", 48, [P, KD, SEQ], F32R)
        xt_lo = sb("xt_lo", 64, [P, KD, SEQ], F32R)
        xw = sb("xw", 96, [P, KD, SEQ])
        xw_hi = sb("xw_hi", 144, [P, KD, SEQ], F32R)
        xw_lo = sb("xw_lo", 160, [P, KD, SEQ], F32R)
        rms_row = sb("rms_row", 176, [P, SEQ])
        rms_diag = sb("rms_diag", 178, [P, TT, P])
        vgs = sb("vgs", 80, [P, 2, TT, D])
        ya_hi = sb("ya_hi", 80, [P, KD, SEQ], F32R)
        ya_lo = sb("ya_lo", 96, [P, KD, SEQ], F32R)
        h = sb("h", 80, [P, TT, D])
        hn = sb("hn", 96, [P, 2, D])
        fw = sb("fw", 108, [P, D])
        xn_in = sb("xn_in", 112, [P, TT, D])
        vbias_bc = sb("vbias_bc", 128, [P, 2, D])
        lnw_bc = sb("lnw_bc", 136, [P, D])
        lnb_bc = sb("lnb_bc", 140, [P, D])
        ya = sb("ya", 112, [P, KD, SEQ])
        yb = sb("yb", 128, [P, KD, SEQ])
        mg_hi = sb("mg_hi", 112, [P, KD, SEQ], F32R)
        mg_lo = sb("mg_lo", 128, [P, KD, SEQ], F32R)
        act = sb("act", 112, [P, KF, SEQ])
        qk = sb("qk", 144, [P, 2 * HEADS, SEQ])
        yb_hi = sb("yb_hi", 144, [P, KD, SEQ], F32R)
        yb_lo = sb("yb_lo", 160, [P, KD, SEQ], F32R)
        htmp = [sb(f"htmp{s}", 144 + 4 * s, [P, 2, 4, P]) for s in range(2)]
        sq_junk0 = sb("sq_junk0", 190, [P, D])
        sq_junk = sb("sq_junk", 160, [P, D])
        sq_junk2 = sb("sq_junk2", 176, [P, D])
        g = sb("g", 160, [P, HEADS, SEQ])
        cum = sb("cum", 168, [P, NCH, CHUNK])
        rest = sb("rest", 170, [P, NCH, CHUNK])
        expb = sb("expb", 172, [P, NCH, CHUNK])
        ah = [sb(f"ah{s}", 160 + 4 * s, [P, 2, SEQ], F32R) for s in range(2)]
        al = [sb(f"al{s}", 168 + 4 * s, [P, 2, SEQ], F32R) for s in range(2)]
        ken = sb("ken", 176, [P, TT, P])
        osq = sb("osq", 176, [P, SEQ])
        sct = sb("sct", 178, [P, TT, P])
        vst = sb("vst", 180, [P, TT, DV])
        vns = sb("vns", 184, [P, TT, DV])
        state = sb("state", 188, [P, NCH - 1, DV])
        rs = sb("rs", 195, [P, SEQ])
        lr_raw = sb("lr_raw", 180, [P, KD, P])
        lr_w = sb("lr_w", 184, [P, KD, P], F32R)
        glr = sb("glr", 192, [P, SEQ], F32R)
        gk2_raw = sb("gk2_raw", 188, [P, HEADS * DK])
        gk2 = sb("gk2", 195, [P, HEADS * DK], F32R)
        zabs = sb("zabs", 180, [P, HEADS, SEQ])
        sg_a = sb("sg_a", 176, [P, 2, SEQ])
        sg_b = sb("sg_b", 180, [P, 2, SEQ])
        prod_a = sb("prod_a", 184, [P, 2, SEQ])
        prod_b = sb("prod_b", 188, [P, 2, SEQ])
        sil = sb("sil", 176, [P, 2, SEQ])
        sgub_bc = sb("sgub_bc", 197, [P, GROUPS, P])
        swt = sb("swt", 201, [P, GROUPS, P])
        ident = sb("ident", 205, [P, P])
        ones_dv = sb("ones_dv", 205.5, [P, P])
        keep = sb("keep", 206, [P, SEQ], BF16)
        causal = sb("causal", 207, [P, P], U8)
        par = sb("par", 207.125, [P, K_END])
        small = sb("small", 207.375, [P, 24])
        ms, sd, rstd = small[:, 0:4], small[:, 4:8], small[:, 8:12]
        eps = small[:, 12:13]
        scores_seen = sb("scores_seen", 207.5, [P, 1])
        warm = [small[:, 13 + n:14 + n] for n in range(2)]
        first_ms, second_sum = small[:, 16:20], small[:, 20:24]
        decay = small[:, 16:24]
        causal_f = sb("causal_f", 194.5, [P, P])
        bnst = sb("bnst", 194, [P, TT, 2, 6])
        bnag = sb("bnag", 194.25, [P, TT, 2])

        bank = [ctx.enter_context(nc.psum_tensor(f"bank{b}", [P, HALF], F32)) for b in range(8)]

        raw_landed = [sem(f"raw_landed{s}") for s in range(2)]
        first_half_low, second_half_low = sem("first_half_low"), sem("second_half_low")
        hi_ready, lo_ready, block_used = sem("hi_ready"), sem("lo_ready"), sem("block_used")
        x_landed = [sem(f"x_landed{t}") for t in range(TT)]
        xt_landed = [sem(f"xt_landed{q}") for q in range(4)]
        first_half_landed, first_half_hi, block0_low = sem("first_half_landed"), sem("first_half_hi"), sem("block0_low")
        weighed, xw_hi_ready, xw_ready = sem("weighed"), sem("xw_hi_ready"), sem("xw_ready")
        diag_ready, row_done, row_ready, xw_scaled = sem("diag_ready"), sem("row_done"), sem("row_ready"), sem("xw_scaled")
        h_landed, fw_landed, lr_landed = sem("h_landed"), sem("fw_landed"), sem("lr_landed")
        par_landed, ident_landed, gk2_landed = sem("par_landed"), sem("ident_landed"), sem("gk2_landed")
        vbias_landed, ln_landed = sem("vbias_landed"), sem("ln_landed")
        sgub_landed, swt_landed, causal_landed = sem("sgub_landed"), sem("swt_landed"), sem("causal_landed")
        eps_set, keep_set, ones_set, sct_zeroed = sem("eps_set"), sem("keep_set"), sem("ones_set"), sem("sct_zeroed")
        causal_set, seen = sem("causal_set"), sem("seen")
        swt_masked = sem("swt_masked")
        sq_sum, sd_ready, rstd_ready, norm_ready = sem("sq_sum"), sem("sd_ready"), sem("rstd_ready"), sem("norm_ready")
        turned, turned_w, xt_hi_ready, xt_ready = sem("turned"), sem("turned_w"), sem("xt_hi_ready"), sem("xt_ready")
        lr_hi_ready, lr_w_ready, lr_done, glr_hi_ready, glr_ready = (
            sem("lr_hi_ready"), sem("lr_w_ready"), sem("lr_done"), sem("glr_hi_ready"), sem("glr_ready"))
        gk2_hi_ready, gk2_ready = sem("gk2_hi_ready"), sem("gk2_ready")
        acc_done, acc_free = sem("acc_done"), sem("acc_free")
        tile_done, tile_free = sem("tile_done"), sem("tile_free")
        z_done, zabs_ready, zexp_ready, zln_ready, zmin_ready, g_ready = (
            sem("z_done"), sem("zabs_ready"), sem("zexp_ready"), sem("zln_ready"), sem("zmin_ready"), sem("g_ready"))
        vgelu_ready, bn_ready, bnag_ready, vsd_ready, vrstd_ready, vnorm_ready, vscaled, vn_ready = (
            sem("vgelu_ready"), sem("bn_ready"), sem("bnag_ready"), sem("vsd_ready"), sem("vrstd_ready"),
            sem("vnorm_ready"), sem("vscaled"), sem("vn_ready"))
        cum_ready, rest_ready, exp_ready, decayed = sem("cum_ready"), sem("rest_ready"), sem("exp_ready"), sem("decayed")
        staged, kend_turned, ken_ready = sem("staged"), sem("kend_turned"), sem("ken_ready")
        scores_done, sct_ready, kv_done, state_ready = sem("scores_done"), sem("sct_ready"), sem("kv_done"), sem("state_ready")
        mixed_done, mixed_biased, ya_ready = sem("mixed_done"), sem("mixed_biased"), sem("ya_ready")
        o_done, sq_ready, osq_ready, ms_done, osd_ready, orstd_ready, yb_scaled, yb_ready = (
            sem("o_done"), sem("sq_ready"), sem("osq_ready"), sem("ms_done"), sem("osd_ready"),
            sem("orstd_ready"), sem("yb_scaled"), sem("yb_ready"))
        y_hi_ready = sem("y_hi_ready")
        branch_done, branch_free, prod_ready, msum_ready, mg_hi_ready = (
            sem("branch_done"), sem("branch_free"), sem("prod_ready"), sem("msum_ready"), sem("mg_hi_ready"))
        gate_done, up_done, sil_ready, act_ready = sem("gate_done"), sem("up_done"), sem("sil_ready"), sem("act_ready")
        ah_ready, al_ready = sem("ah_ready"), sem("al_ready")
        first_ms_ready = sem("first_ms_ready")
        h0_low = sem("h0_low")
        y_ready, y_stored = sem("y_ready"), sem("y_stored")

        block = ctx.enter_context(nc.Block())

        def wk(t, s):
            return t[s][:, :].rearrange("p (k n) -> p k n", k=KD)

        def wn(t, s):
            return t[s][:, :].rearrange("p (k n) -> p k n", k=2)

        @block.sync
        def _(sp):
            sp.dma_start(xw[:, 0:2, :], x_t[:, 0:2, :]).then_inc(xt_landed[0], 16)
            sp.dma_start(raw[0][:, 0:D], wstream[0][:, 0:D]).then_inc(first_half_landed, 16)
            sp.dma_start(raw[0][:, D:BLK], wstream[0][:, D:BLK]).then_inc(raw_landed[0], 16)
            sp.dma_start(xw[:, 2:4, :], x_t[:, 2:4, :]).then_inc(xt_landed[1], 16)
            sp.dma_start(raw[1][:, :], wstream[1]).then_inc(raw_landed[1], 16)
            for q in range(2, 4):
                sp.dma_start(xw[:, 2 * q:2 * q + 2, :], x_t[:, 2 * q:2 * q + 2, :]).then_inc(xt_landed[q], 16)
            sp.dma_start(swt[:, :, :], sgu_wt).then_inc(swt_landed, 16)
            for t in range(2):
                sp.dma_start(xn_in[:, t, :], x[t * P:(t + 1) * P, :]).then_inc(x_landed[t], 16)
            sp.wait_ge(block0_low, 1)
            with sp.Fori(1, N_BLKS // 2) as i:
                for s in range(2):
                    sp.wait_ge(hi_ready, i * 2 + (s - 1))
                    sp.wait_ge(lo_ready, i * 2 + (s - 1))
                    sp.dma_start(raw[s][:, :], wstream[bass.ds(i * 2 + s, 1)].rearrange("a p n -> (a p) n")
                                 ).then_inc(raw_landed[s], 16)
            sp.wait_ge(hi_ready, N_BLKS - 2)
            sp.wait_ge(lo_ready, N_BLKS - 2)
            sp.dma_start(raw[0][:, :], wstream[N_BLKS - 1]).then_inc(raw_landed[0], 16)
            for t in range(TT - 1):
                sp.wait_ge(y_ready, 2 * t + 2)
                sp.dma_start(out[t * P:(t + 1) * P, :], h[:, t, :]).then_inc(y_stored, 16)
            for hf in range(2):
                sp.wait_ge(y_ready, 2 * TT - 1 + hf)
                hs = slice(hf * HALF, (hf + 1) * HALF)
                sp.dma_start(out[(TT - 1) * P:TT * P, hs], h[:, TT - 1, hs]).then_inc(y_stored, 16)
            sp.wait_ge(y_stored, 16 * (TT + 1))

        @block.gpsimd
        def _(pool):
            def low(b, s, landed):
                pool.wait_ge(raw_landed[s], landed)
                pool.wait_ge(hi_ready, b + 1)
                pool.tensor_tensor(w_lo[s][:, :], raw[s][:, :], w_hi[s][:, :], ALU.subtract).then_inc(lo_ready, 1)

            def low_shared(b, s, landed):
                pool.wait_ge(raw_landed[s], landed)
                pool.wait_ge(hi_ready, b + 1)
                pool.tensor_tensor(w_lo[s][:, 0:D], raw[s][:, 0:D], w_hi[s][:, 0:D], ALU.subtract
                                   ).then_inc(first_half_low, 1)
                pool.wait_ge(first_half_low, 1)
                pool.wait_ge(second_half_low, 1)
                pool.sem_inc(lo_ready, 1)

            pool.wait_ge(raw_landed[0], 16)
            pool.wait_ge(hi_ready, 1)
            pool.tensor_tensor(w_lo[0][:, D:BLK], raw[0][:, D:BLK], w_hi[0][:, D:BLK], ALU.subtract).then_inc(lo_ready, 1)
            low(1, 1, 16)
            pool.wait_ge(swt_landed, 16)
            pool.affine_select(out=swt[:, :, :], in_=swt[:, :, :], compare_op=ALU.is_ge, fill=0.0, base=0,
                               pattern=[[0, GROUPS], [1, P]], channel_multiplier=-1).then_inc(swt_masked, 1)
            with pool.Fori(1, B_FFN // 2) as i:
                for s in range(2):
                    low(i * 2 + s, s, i * 16 + 16)
            low(B_FFN, 0, 8 * B_FFN + 16)
            for hf in range(2):
                pool.wait_ge(xt_hi_ready, 4 + hf + 1)
                pool.tensor_tensor(xt_lo[:, 4 * hf:4 * hf + 4, 0:P], htmp[0][:, hf],
                                   xt_hi[:, 4 * hf:4 * hf + 4, 0:P], ALU.subtract).then_inc(h0_low, 1)
            low(B_FFN + 1, 1, 8 * B_FFN + 16)
            low_shared(B_FFN + 2, 0, 8 * (B_FFN + 4))
            low(B_FFN + 3, 1, 8 * (B_FFN + 4))
            with pool.Fori(B_FFN // 2 + 2, N_BLKS // 2) as i:
                for s in range(2):
                    low(i * 2 + s, s, i * 16 + 16)
            low(N_BLKS - 1, 0, 16 * (N_BLKS // 2 + 1))

        @block.scalar
        def _(a):
            a.dma_start(par[:, :], cols).then_inc(par_landed, 16)
            a.dma_start(ident[:, :], ident_d).then_inc(ident_landed, 16)

            def high(b, s, landed):
                a.wait_ge(raw_landed[s], landed)
                a.activation(w_hi[s][:, :], raw[s][:, :], ACT.Copy).then_inc(hi_ready, 1)

            def high2(b, s, used, n):
                a.wait_ge(used, n)
                high(b, s, (b - s) * 8 + 16)

            def stats(src, t, junk, n0):
                a.activation(junk[:, :], src, ACT.Square, accum_out=ms[:, t:t + 1]).then_inc(sq_sum, 1)
                a.wait_ge(sq_sum, n0 + t + 1)
                a.activation(sd[:, t:t + 1], ms[:, t:t + 1], ACT.Sqrt, bias=eps, scale=1.0 / D).then_inc(sd_ready, 1)

            def split_turned(tmp, t):
                for hf in range(2):
                    a.wait_ge(turned_w, 2 * t + hf + 1)
                    a.activation(xt_hi[:, 4 * hf:4 * hf + 4, t * P:(t + 1) * P], tmp[:, hf], ACT.Copy
                                 ).then_inc(xt_hi_ready, 1)

            def x_high(q):
                a.wait_ge(weighed, 2 * q + 2)
                a.activation(xw_hi[:, 2 * q:2 * q + 2, :], xw[:, 2 * q:2 * q + 2, :], ACT.Copy).then_inc(xw_hi_ready, 1)

            x_high(0)
            a.wait_ge(first_half_landed, 16)
            a.activation(w_hi[0][:, 0:D], raw[0][:, 0:D], ACT.Copy).then_inc(first_half_hi, 1)
            a.wait_ge(raw_landed[0], 16)
            a.activation(w_hi[0][:, D:BLK], raw[0][:, D:BLK], ACT.Copy).then_inc(hi_ready, 1)
            x_high(1)
            high(1, 1, 16)
            x_high(2)
            x_high(3)
            a.wait_ge(eps_set, 1)
            for j in range(2):
                high2(2 + j, j, block_used, j + 1)
                if j == 0:
                    for t in range(2, TT):
                        a.dma_start(xn_in[:, t, :], x[t * P:(t + 1) * P, :]).then_inc(x_landed[t], 16)
                    a.dma_start(vbias_bc[:, :, :].rearrange("p a n -> p (a n)"), vbias.partition_broadcast(P)).then_inc(vbias_landed, 16)
                for t in (2 * j, 2 * j + 1):
                    a.wait_ge(x_landed[t], 16)
                    stats(xn_in[:, t, :], t, sq_junk0, 0)
            a.dma_start(lr_raw[:, :, :], w_lr).then_inc(lr_landed, 16)
            a.dma_start(gk2_raw[:, :], w_gk2).then_inc(gk2_landed, 16)
            a.dma_start(causal_f[:, :], causal_d).then_inc(causal_landed, 16)
            a.dma_start(lnw_bc[:, :], lnw.partition_broadcast(P)).then_inc(ln_landed, 16)
            a.dma_start(lnb_bc[:, :], lnb.partition_broadcast(P)).then_inc(ln_landed, 16)
            a.dma_start(sgub_bc[:, :, :].rearrange("p g t -> p (g t)"), sgub.partition_broadcast(P)).then_inc(sgub_landed, 16)
            high2(4, 0, block_used, 3)
            high2(5, 1, acc_done, 8)
            a.wait_ge(row_done, 1)
            a.activation(rms_row[:, :], bank[0][:, :], ACT.Copy).then_inc(row_ready, 1)
            for q in range(4):
                a.wait_ge(xw_scaled, 2 * q + 2)
                a.activation(xt_hi[:, 2 * q:2 * q + 2, :], xw[:, 2 * q:2 * q + 2, :], ACT.Copy).then_inc(xt_hi_ready, 1)
            a.wait_ge(lr_landed, 16)
            a.activation(lr_w[:, :, :], lr_raw[:, :, :], ACT.Copy).then_inc(lr_hi_ready, 1)
            a.wait_ge(gk2_landed, 16)
            a.activation(gk2[:, :], gk2_raw[:, :], ACT.Copy).then_inc(gk2_hi_ready, 1)
            for j in range(3):
                high2(6 + j, j % 2, block_used, 3 + j + 1)
            high2(9, 1, acc_done, 16)

            for t in range(TT):
                a.wait_ge(acc_free, 8 + 8 + 2 * t + 2)
                a.activation(vgs[:, 1, t, :], vgs[:, 1, t, :], ACT.Gelu_apprx_tanh).then_inc(vgelu_ready, 1)
            a.wait_ge(lr_done, 1)
            a.activation(glr[:, :], bank[4][:, :], ACT.Identity, bias=par[:, K_LR:K_LR + 1]).then_inc(glr_hi_ready, 1)

            def queries_or_keys(i):
                for j in range(2):
                    for t in range(2):
                        n = 2 * j + t
                        a.wait_ge(tile_done, i * 4 + (n + 1))
                        a.activation(qk[:, i * 4 + n, :], bank[n][:, :], ACT.Identity,
                                     bias=par[:, i * 4 + (K_QK + n):i * 4 + (K_QK + n) + 1]).then_inc(tile_free, 1)
                    high2(i * 2 + (B_QK + 2 + j), j, tile_done, i * 4 + (2 * j + 2))

            queries_or_keys(0)
            for hd in range(HEADS):
                a.wait_ge(z_done, hd + 1)
                a.activation(zabs[:, hd, :], bank[4 + hd][:, :], ACT.Abs, bias=par[:, K_BGK + hd:K_BGK + hd + 1]
                             ).then_inc(zabs_ready, 1)
            a.wait_ge(zabs_ready, HEADS)
            a.activation(zabs[:, :, :], zabs[:, :, :], ACT.Exp, scale=-1.0).then_inc(zexp_ready, 1)
            a.wait_ge(zexp_ready, 1)
            a.activation(zabs[:, :, :], zabs[:, :, :], ACT.Ln, bias=1.0).then_inc(zln_ready, 1)
            a.wait_ge(bnag_ready, TT)
            a.activation(sd[:, :].unsqueeze(2), bnag[:, :, 1:2], ACT.Sqrt, bias=eps).then_inc(vsd_ready, 1)
            queries_or_keys(1)

            with a.Fori(0, HEADS) as i:
                def silu_r(t):
                    a.wait_ge(tile_done, i * 4 + (8 + t + 1))
                    a.activation(yb[:, bass.ds(i * 2 + t, 1), :], bank[t][:, :].unsqueeze(1), ACT.Silu,
                                 bias=par[:, bass.ds(i * 2 + (K_R + t), 1)]).then_inc(tile_free, 1)

                silu_r(0)
                a.wait_ge(cum_ready, i + 1)
                a.activation(expb[:, :, :], cum[:, :, :], ACT.Exp, scale=1.0 / GATE_NORM).then_inc(exp_ready, 1)
                a.wait_ge(rest_ready, i + 1)
                a.activation(rest[:, :, :], rest[:, :, :], ACT.Exp, scale=1.0 / GATE_NORM).then_inc(exp_ready, 1)
                a.activation(cum[:, :, :], cum[:, :, :], ACT.Exp, scale=-1.0 / GATE_NORM).then_inc(exp_ready, 1)
                a.wait_ge(vn_ready, 2 * TT)
                a.activation(vst[:, :, :], vgs[:, 0, :, bass.ds(i * DV, DV)], ACT.Copy).then_inc(staged, 1)
                a.activation(vns[:, :, :], vgs[:, 1, :, bass.ds(i * DV, DV)], ACT.Copy).then_inc(staged, 1)
                silu_r(1)
                high2(i * 2 + (B_RU + 2), 0, tile_done, i * 4 + 10)
                a.wait_ge(tile_done, i * 4 + 11)
                a.activation(ya[:, bass.ds(i * 2, 1), :], bank[0][:, :].unsqueeze(1), ACT.Gelu_apprx_tanh,
                             bias=par[:, bass.ds(i * 2 + K_U, 1)]).then_inc(tile_free, 1)
                a.wait_ge(kend_turned, i + 1)
                a.activation(ken[:, :, :], bank[4][:, :], ACT.Copy).then_inc(ken_ready, 1)
                a.wait_ge(tile_done, i * 4 + 12)
                a.activation(ya[:, bass.ds(i * 2 + 1, 1), :], bank[1][:, :].unsqueeze(1), ACT.Gelu_apprx_tanh,
                             bias=par[:, bass.ds(i * 2 + (K_U + 1), 1)]).then_inc(tile_free, 1)
                high2(i * 2 + (B_RU + 3), 1, tile_done, i * 4 + 12)
                a.wait_ge(o_done, i * 2 + 1)
                a.activation(osq[:, :], bank[6][:, :], ACT.Square).then_inc(sq_ready, 1)
                a.wait_ge(o_done, i * 2 + 2)
                a.activation(rs[:, :], bank[7][:, :], ACT.Square).then_inc(sq_ready, 1)
                a.wait_ge(ms_done, i + 1)
                a.activation(rs[:, :], bank[2][:, :], ACT.Sqrt, bias=eps).then_inc(osd_ready, 1)

            a.wait_ge(ya_ready, KD)
            for q in range(2):
                a.activation(ya_hi[:, 4 * q:4 * q + 4, :], ya[:, 4 * q:4 * q + 4, :], ACT.Copy).then_inc(y_hi_ready, 1)
            for q in range(2):
                a.wait_ge(yb_ready, 4 * q + 4)
                a.activation(yb_hi[:, 4 * q:4 * q + 4, :], yb[:, 4 * q:4 * q + 4, :], ACT.Copy).then_inc(y_hi_ready, 1)
            with a.Fori(0, KD // 2) as i:
                for j, (sg, kc) in enumerate(((sg_a, K_GA), (sg_b, K_GB))):
                    for t in range(2):
                        a.wait_ge(tile_done, i * 4 + (24 + 2 * j + t + 1))
                        a.activation(sg[:, t, :], bank[2 * j + t][:, :], ACT.Sigmoid,
                                     bias=par[:, bass.ds(i * 2 + (kc + t), 1)]).then_inc(tile_free, 1)
                    high2(i * 4 + (B_MERGE + 2 + j), j, tile_done, i * 4 + (24 + 2 * j + 2))
                high2(i * 4 + (B_MERGE + 4), 0, branch_done, i * 4 + 2)
                high2(i * 4 + (B_MERGE + 5), 1, branch_done, i * 4 + 4)
                for t in range(2):
                    a.wait_ge(msum_ready, i * 2 + (t + 1))
                    a.activation(mg_hi[:, bass.ds(i * 2 + t, 1), :], prod_a[:, t:t + 1, :], ACT.Copy
                                 ).then_inc(mg_hi_ready, 1)

            a.wait_ge(branch_done, 2 * KD)
            a.dma_start(h[:, :, :], x.rearrange("(t p) n -> p t n", p=P)).then_inc(h_landed, 16)
            a.dma_start(fw[:, :], finalw.partition_broadcast(P)).then_inc(fw_landed, 16)
            for j in range(3):
                high2(B_OUT + 2 + j, j % 2, block_used, 6 + j + 1)
            a.activation(warm[0], eps, ACT.Sqrt)

            def stats_h(t):
                a.wait_ge(acc_free, 24 + 2 * t + 2)
                stats(h[:, t, :], t, sq_junk, TT)

            def normalise_h(t):
                a.wait_ge(rstd_ready, TT + t + 1)
                if t >= 2:
                    a.wait_ge(turned, 2 * (t - 1))
                a.activation(hn[:, t % 2, :], h[:, t, :], ACT.Identity, scale=rstd[:, t:t + 1]).then_inc(norm_ready, 1)

            stats_h(0)
            normalise_h(0)
            stats_h(1)
            normalise_h(1)
            split_turned(htmp[0], 0)
            split_turned(htmp[1], 1)
            high2(B_FFN + 1, 1, acc_done, 24)
            stats_h(2)
            normalise_h(2)
            stats_h(3)
            normalise_h(3)
            split_turned(htmp[0], 2)
            split_turned(htmp[1], 3)

            def gates(i, first=False):
                for t in range(2):
                    a.wait_ge(gate_done, i * 2 + (t + 1))
                    if not first:
                        a.wait_ge(act_ready, i * 2 + (t - 1))
                    a.activation(sil[:, t, :], bank[t][:, :], ACT.Silu).then_inc(sil_ready, 1)
                high2(i * 2 + (B_FFN + 2), 0, gate_done, i * 2 + 2)
                high2(i * 2 + (B_FFN + 3), 1, up_done, i * 2 + 2)

            def act_high(m, s):
                a.activation(ah[s][:, :, :], act[:, bass.ds(m * 2, 2), :], ACT.Copy).then_inc(ah_ready, 1)

            gates(0, True)
            a.wait_ge(act_ready, 2)
            act_high(0, 0)
            with a.Fori(1, FFN_IT) as i:
                gates(i)
            act_high(1, 1)
            high2(B_DOWN + 2, 0, block_used, 9 + 1)
            a.wait_ge(act_ready, KF)
            act_high(2, 0)
            with a.Fori(0, 4) as i:
                for s in range(2):
                    high2(i * 2 + (B_DOWN + 3 + s), 1 - s, block_used, i * 2 + (9 + 2 + s))
                    act_high(i * 2 + (3 + s), 1 - s)
            a.activation(warm[1], eps, ACT.Sqrt)
            for t in range(TT):
                a.wait_ge(acc_free, 32 + 2 * t + 1)
                a.activation(sq_junk2[:, 0:HALF], h[:, t, 0:HALF], ACT.Square, accum_out=ms[:, t:t + 1]).then_inc(sq_sum, 1)
                a.wait_ge(sq_sum, 2 * TT + 2 * t + 1)
                a.activation(first_ms[:, t:t + 1], ms[:, t:t + 1], ACT.Identity, bias=eps, scale=1.0 / D
                             ).then_inc(first_ms_ready, 1)
                a.wait_ge(acc_free, 32 + 2 * t + 2)
                a.activation(sq_junk2[:, HALF:D], h[:, t, HALF:D], ACT.Square, accum_out=second_sum[:, t:t + 1]).then_inc(sq_sum, 1)
                a.wait_ge(sq_sum, 2 * TT + 2 * t + 2)
                a.wait_ge(first_ms_ready, t + 1)
                a.activation(sd[:, t:t + 1], second_sum[:, t:t + 1], ACT.Sqrt, bias=first_ms[:, t:t + 1], scale=1.0 / D
                             ).then_inc(sd_ready, 1)

        @block.vector
        def _(v):
            v.memset(eps, EPS).then_inc(eps_set, 1)
            v.memset(keep[:, :], 1.0).then_inc(keep_set, 1)
            v.memset(ones_dv[:, :], 1.0 / DV).then_inc(ones_set, 1)
            v.wait_ge(keep_set, 1)
            v.memset(keep[:, :].rearrange("p (c t) -> p c t", t=CHUNK)[:, :, 0:1], 0.0).then_inc(keep_set, 1)
            v.wait_ge(par_landed, 16)

            def weigh_turned(tmp, t):
                for hf in range(2):
                    n = 2 * t + hf
                    v.wait_ge(turned, n + 1)
                    if t == 2:
                        v.wait_ge(h0_low, hf + 1)
                    elif t == 3:
                        v.wait_ge(xt_ready, 4 + hf + 1)
                    w = par[:, K_N2 + 4 * hf:K_N2 + 4 * hf + 4].unsqueeze(2).broadcast_to([P, 4, P])
                    v.tensor_tensor(tmp[:, hf], bank[2 * t + hf][:, :].rearrange("p (k t) -> p k t", k=4), w, ALU.mult
                                    ).then_inc(turned_w, 1)

            def low_turned(tmp, t):
                for hf in range(2):
                    v.wait_ge(xt_hi_ready, 4 + 2 * t + hf + 1)
                    v.tensor_tensor(xt_lo[:, 4 * hf:4 * hf + 4, t * P:(t + 1) * P], tmp[:, hf],
                                    xt_hi[:, 4 * hf:4 * hf + 4, t * P:(t + 1) * P], ALU.subtract).then_inc(xt_ready, 1)

            def low_second_half(b, s, landed):
                v.wait_ge(raw_landed[s], landed)
                v.wait_ge(hi_ready, b + 1)
                v.tensor_tensor(w_lo[s][:, D:BLK], raw[s][:, D:BLK], w_hi[s][:, D:BLK], ALU.subtract
                                ).then_inc(second_half_low, 1)

            for q in range(4):
                v.wait_ge(xt_landed[q], 16)
                for k in (2 * q, 2 * q + 1):
                    v.tensor_scalar(xw[:, k, :], xw[:, k, :], par[:, K_N1 + k:K_N1 + k + 1], None, ALU.mult
                                    ).then_inc(weighed, 1)
                v.wait_ge(xw_hi_ready, q + 1)
                ks = slice(2 * q, 2 * q + 2)
                v.tensor_tensor(xw_lo[:, ks, :], xw[:, ks, :], xw_hi[:, ks, :], ALU.subtract).then_inc(xw_ready, 1)
                if q == 0:
                    v.wait_ge(first_half_hi, 1)
                    v.tensor_tensor(w_lo[0][:, 0:D], raw[0][:, 0:D], w_hi[0][:, 0:D], ALU.subtract).then_inc(block0_low, 1)
            v.wait_ge(ident_landed, 16)
            for t in range(TT):
                v.wait_ge(sd_ready, t + 1)
                v.reciprocal(rstd[:, t:t + 1], sd[:, t:t + 1]).then_inc(rstd_ready, 1)
                v.wait_ge(rstd_ready, t + 1)
                v.tensor_scalar(rms_diag[:, t, :], ident[:, :], rstd[:, t:t + 1], float(DV), ALU.mult, ALU.mult
                                ).then_inc(diag_ready, 1)
            v.wait_ge(vbias_landed, 16)

            def values(i):
                for t in range(TT):
                    for hf in range(2):
                        v.wait_ge(acc_done, i * 8 + (2 * t + hf + 1))
                        cs = slice(hf * HALF, (hf + 1) * HALF)
                        v.scalar_tensor_tensor(vgs[:, i, t, cs], bank[2 * t + hf][:, :], rstd[:, t:t + 1],
                                               vbias_bc[:, i, cs], ALU.mult, ALU.add).then_inc(acc_free, 1)

            values(0)
            v.wait_ge(row_ready, 1)
            for k in range(KD):
                v.tensor_tensor(xw[:, k, :], xw[:, k, :], rms_row[:, :], ALU.mult).then_inc(xw_scaled, 1)
            for q in range(4):
                ks = slice(2 * q, 2 * q + 2)
                v.wait_ge(xt_hi_ready, q + 1)
                v.tensor_tensor(xt_lo[:, ks, :], xw[:, ks, :], xt_hi[:, ks, :], ALU.subtract).then_inc(xt_ready, 1)
            v.wait_ge(lr_hi_ready, 1)
            c3, c2 = slice(96, 96 + LOWRANK), slice(64, 64 + LOWRANK)
            v.tensor_tensor(lr_w[:, :, c3], lr_raw[:, :, c3], lr_w[:, :, c3], ALU.subtract).then_inc(lr_w_ready, 1)
            v.wait_ge(gk2_hi_ready, 1)
            v.tensor_tensor(gk2[c2, :], gk2_raw[c2, :], gk2[c2, :], ALU.subtract).then_inc(gk2_ready, 1)
            v.wait_ge(causal_landed, 16)
            v.tensor_copy(causal[:, :], causal_f[:, :]).then_inc(causal_set, 1)
            v.wait_ge(row_done, 1)
            v.memset(sct[:, :, :], 0.0).then_inc(sct_zeroed, 1)
            v.wait_ge(xt_ready, 4)
            values(1)

            v.wait_ge(glr_hi_ready, 1)
            c1 = slice(32, 32 + LOWRANK)
            v.scalar_tensor_tensor(glr[c1, :], bank[4][c1, :], par[c1, K_LR:K_LR + 1], glr[c1, :],
                                   ALU.add, ALU.subtract).then_inc(glr_ready, 1)
            for t in range(TT):
                v.wait_ge(vgelu_ready, t + 1)
                for hf in range(2):
                    v.bn_stats(bnst[:, t, hf, :], vgs[:, 1, t, hf * HALF:(hf + 1) * HALF]).then_inc(bn_ready, 1)
                v.wait_ge(bn_ready, 2 * t + 2)
                v.bn_aggr(bnag[:, t, :], bnst[:, t, :, :]).then_inc(bnag_ready, 1)
            for hd in range(HEADS):
                v.wait_ge(zabs_ready, hd + 1)
                v.tensor_scalar(g[:, hd, :], bank[4 + hd][:, :], par[:, K_BGK + hd:K_BGK + hd + 1], 0.0,
                                ALU.add, ALU.min).then_inc(zmin_ready, 1)
            v.wait_ge(zln_ready, 1)
            v.wait_ge(zmin_ready, HEADS)
            v.tensor_tensor(g[:, :, :], g[:, :, :], zabs[:, :, :], ALU.subtract).then_inc(g_ready, 1)
            v.wait_ge(vsd_ready, 1)
            v.reciprocal(rstd[:, :], sd[:, :]).then_inc(vrstd_ready, 1)
            v.wait_ge(vrstd_ready, 1)
            v.wait_ge(ln_landed, 32)
            for t in range(TT):
                v.tensor_scalar(vgs[:, 1, t, :], vgs[:, 1, t, :], bnag[:, t, 0:1], rstd[:, t:t + 1],
                                ALU.subtract, ALU.mult).then_inc(vnorm_ready, 1)
            for t in range(TT):
                v.wait_ge(vnorm_ready, t + 1)
                v.tensor_tensor(vgs[:, 1, t, :], vgs[:, 1, t, :], lnw_bc[:, :], ALU.mult).then_inc(vscaled, 1)
            for t in range(TT):
                v.wait_ge(vscaled, t + 1)
                v.tensor_tensor(vgs[:, 1, t, :], vgs[:, 1, t, :], lnb_bc[:, :], ALU.add).then_inc(vn_ready, 2)

            v.wait_ge(g_ready, 1)
            v.wait_ge(keep_set, 2)
            v.wait_ge(sct_zeroed, 1)
            v.wait_ge(sgub_landed, 16)
            v.wait_ge(causal_set, 1)
            with v.Fori(0, HEADS) as i:
                v.tensor_tensor_scan(cum[:, :, :].rearrange("p c t -> p (c t)"), keep[:, :],
                                     g[:, bass.ds(i, 1), :].rearrange("p a t -> p (a t)"), 0.0,
                                     ALU.mult, ALU.add).then_inc(cum_ready, 1)
                v.wait_ge(cum_ready, i + 1)
                v.tensor_tensor(rest[:, :, :], cum[:, :, CHUNK - 1:CHUNK].broadcast_to([P, NCH, CHUNK]), cum[:, :, :],
                                ALU.subtract).then_inc(rest_ready, 1)
                v.wait_ge(exp_ready, i * 3 + 1)
                v.wait_ge(tile_free, 4 + 8)
                v.tensor_copy(decay.unsqueeze(2), expb[:, :, CHUNK - 1:CHUNK]).then_inc(decayed, 1)
                v.wait_ge(decayed, i * 4 + 1)
                v.scalar_tensor_tensor(expb[:, :, :].rearrange("p c t -> p (c t)"),
                                       qk[:, bass.ds(i, 1), :].rearrange("p a t -> p (a t)"), DK ** -0.5,
                                       expb[:, :, :].rearrange("p c t -> p (c t)"), ALU.mult, ALU.mult).then_inc(decayed, 1)
                v.wait_ge(exp_ready, i * 3 + 2)
                kh = qk[:, bass.ds(i + HEADS, 1), :].rearrange("p a (c t) -> p (a c) t", t=CHUNK)
                v.tensor_tensor(rest[:, :, :], kh, rest[:, :, :], ALU.mult).then_inc(decayed, 1)
                v.wait_ge(exp_ready, i * 3 + 3)
                v.tensor_tensor(cum[:, :, :], kh, cum[:, :, :], ALU.mult).then_inc(decayed, 1)

                v.wait_ge(scores_done, i + 1)
                v.memset(scores_seen[:, :], 0.0).then_inc(seen, 1)
                v.copy_predicated(sct[:, :, :], causal[:, :].unsqueeze(1).broadcast_to([P, TT, P]),
                                  bank[5][:, :].rearrange("p (t s) -> p t s", t=TT)).then_inc(sct_ready, 1)

                for n in range(NCH - 1):
                    if n % 2 == 0:
                        v.wait_ge(kv_done, i * 4 + (n // 2 + 1))
                    kv = bank[KV_BANKS[n % 4]][:, 0:DV]
                    if n == 0:
                        v.tensor_copy(state[:, 0, :], kv).then_inc(state_ready, 1)
                    else:
                        v.wait_ge(state_ready, i * 7 + n)
                        v.scalar_tensor_tensor(state[:, n, :], state[:, n - 1, :], decay[:, n:n + 1], kv,
                                               ALU.mult, ALU.add).then_inc(state_ready, 1)

                def gate_mixed(q):
                    v.wait_ge(mixed_done, i * 2 + (q + 1))
                    m = bank[4 - q][:, :].rearrange("p (n t) -> p n t", n=TT)
                    v.tensor_tensor(m, m, sgub_bc[:, bass.ds(i * 2 + q, 1), :].broadcast_to([P, TT, P]), ALU.add
                                    ).then_inc(mixed_biased, 1)
                    v.wait_ge(mixed_biased, i * 2 + (q + 1))
                    v.wait_ge(tile_free, i * 4 + (4 + 8 + 3 + q))
                    yg = ya[:, bass.ds(i * 2 + q, 1), :].rearrange("p a t -> p (a t)")
                    v.tensor_tensor(yg, yg, bank[4 - q][:, :], ALU.mult).then_inc(ya_ready, 1)

                v.wait_ge(sq_ready, i * 2 + 2)
                v.tensor_tensor(osq[:, :], osq[:, :], rs[:, :], ALU.add).then_inc(osq_ready, 1)
                gate_mixed(0)
                gate_mixed(1)
                for q in range(2):
                    yh = yb[:, bass.ds(i * 2 + q, 1), :].rearrange("p a t -> p (a t)")
                    v.scalar_tensor_tensor(yh, bank[6 + q][:, :], par[:, K_GN + q:K_GN + q + 1], yh, ALU.mult, ALU.mult
                                           ).then_inc(yb_scaled, 1)
                v.wait_ge(osd_ready, i + 1)
                v.reciprocal(rs[:, :], rs[:, :]).then_inc(orstd_ready, 1)
                v.wait_ge(orstd_ready, i + 1)
                v.wait_ge(yb_scaled, i * 2 + 2)
                for q in range(2):
                    yh = yb[:, bass.ds(i * 2 + q, 1), :].rearrange("p a t -> p (a t)")
                    v.tensor_tensor(yh, yh, rs[:, :], ALU.mult).then_inc(yb_ready, 1)

            for q in range(2):
                ks = slice(4 * q, 4 * q + 4)
                v.wait_ge(y_hi_ready, q + 1)
                v.tensor_tensor(ya_lo[:, ks, :], ya[:, ks, :], ya_hi[:, ks, :], ALU.subtract)
            v.wait_ge(y_hi_ready, 3)
            v.tensor_tensor(yb_lo[:, 0:4, :], yb[:, 0:4, :], yb_hi[:, 0:4, :], ALU.subtract)
            v.wait_ge(y_hi_ready, 4)
            v.tensor_tensor(yb_lo[:, 4:8, :], yb[:, 4:8, :], yb_hi[:, 4:8, :], ALU.subtract).then_inc(branch_free, 1)

            with v.Fori(0, KD // 2) as i:
                v.wait_ge(tile_free, i * 4 + (4 + 24 + 4))
                for q in range(2):
                    v.wait_ge(branch_done, i * 4 + (q + 1))
                    v.tensor_tensor(prod_a[:, q, :], bank[4 + q][:, :], sg_a[:, q, :], ALU.mult).then_inc(prod_ready, 1)
                for q in range(2):
                    v.wait_ge(branch_done, i * 4 + (q + 3))
                    v.tensor_tensor(prod_b[:, q, :], bank[6 + q][:, :], sg_b[:, q, :], ALU.mult).then_inc(prod_ready, 1)
                for q in range(2):
                    v.wait_ge(prod_ready, i * 4 + (q + 3))
                    v.tensor_tensor(prod_a[:, q, :], prod_a[:, q, :], prod_b[:, q, :], ALU.add).then_inc(msum_ready, 1)
                for q in range(2):
                    v.wait_ge(mg_hi_ready, i * 2 + (q + 1))
                    v.tensor_tensor(mg_lo[:, bass.ds(i * 2 + q, 1), :], prod_a[:, q:q + 1, :],
                                    mg_hi[:, bass.ds(i * 2 + q, 1), :], ALU.subtract).then_inc(branch_free, 1)

            def residual(t, n0):
                for hf in range(2):
                    v.wait_ge(acc_done, n0 + 2 * t + hf + 1)
                    hs = h[:, t, hf * HALF:(hf + 1) * HALF]
                    v.tensor_tensor(hs, bank[2 * t + hf][:, :], hs, ALU.add).then_inc(acc_free, 1)

            v.wait_ge(h_landed, 16)

            def rstd_h(t):
                v.wait_ge(sd_ready, TT + t + 1)
                v.reciprocal(rstd[:, t:t + 1], sd[:, t:t + 1]).then_inc(rstd_ready, 1)

            residual(0, 16)
            rstd_h(0)
            residual(1, 16)
            rstd_h(1)
            weigh_turned(htmp[0], 0)
            residual(2, 16)
            weigh_turned(htmp[1], 1)
            low_turned(htmp[1], 1)
            rstd_h(2)
            residual(3, 16)
            rstd_h(3)
            weigh_turned(htmp[0], 2)
            low_turned(htmp[0], 2)
            weigh_turned(htmp[1], 3)
            low_turned(htmp[1], 3)

            def gated(i):
                for t in range(2):
                    v.wait_ge(sil_ready, i * 2 + (t + 1))
                    v.wait_ge(up_done, i * 2 + (t + 1))
                    v.tensor_tensor(act[:, bass.ds(i * 2 + t, 1), :], bank[2 + t][:, :].unsqueeze(1),
                                    sil[:, t:t + 1, :], ALU.mult).then_inc(act_ready, 1)

            def act_low(m, s):
                v.wait_ge(ah_ready, m + 1)
                v.tensor_tensor(al[s][:, :, :], act[:, bass.ds(m * 2, 2), :], ah[s][:, :, :], ALU.subtract
                                ).then_inc(al_ready, 1)

            low_second_half(B_FFN + 2, 0, 8 * (B_FFN + 4))
            gated(0)
            act_low(0, 0)
            with v.Fori(1, FFN_IT) as i:
                gated(i)
            act_low(1, 1)
            act_low(2, 0)
            with v.Fori(0, 4) as i:
                for s in range(2):
                    act_low(i * 2 + (3 + s), 1 - s)
            v.wait_ge(fw_landed, 16)

            def finish(t):
                v.wait_ge(sd_ready, 2 * TT + t + 1)
                v.reciprocal(rstd[:, t:t + 1], sd[:, t:t + 1]).then_inc(rstd_ready, 1)
                v.wait_ge(rstd_ready, 2 * TT + t + 1)
                for hf in range(2):
                    hs = slice(hf * HALF, (hf + 1) * HALF)
                    v.scalar_tensor_tensor(h[:, t, hs], h[:, t, hs], rstd[:, t:t + 1], fw[:, hs], ALU.mult, ALU.mult
                                           ).then_inc(y_ready, 1)

            residual(0, 24)
            finish(0)
            residual(1, 24)
            residual(2, 24)
            finish(1)
            residual(3, 24)
            finish(2)
            finish(3)

        @block.tensor
        def _(pe):
            def turn(src, dst0, t):
                pe.wait_ge(norm_ready, t + 1)
                for hf in range(2):
                    for k in range(4):
                        c = (4 * hf + k) * P
                        last = pe.transpose(bank[dst0 + hf][:, k * P:(k + 1) * P], src[:, c:c + P], ident[:, :])
                    last.then_inc(turned, 1)

            def arrived(b):
                pe.wait_ge(hi_ready, b + 1)
                pe.wait_ge(lo_ready, b + 1)

            def tile_T(dst, wh, wl, t, rh, rl, ts=slice(0, SEQ)):
                cs = slice(t * P, (t + 1) * P)
                for k in range(KD):
                    pe.matmul(dst, wh[:, k, cs], rh[:, k, ts], start=(k == 0), stop=False)
                    pe.matmul(dst, wh[:, k, cs], rl[:, k, ts], start=False, stop=False)
                    last = pe.matmul(dst, wl[:, k, cs], rh[:, k, ts], start=False, stop=(k == KD - 1))
                return last

            def block_N(s, lh, ll, first, last, before=None, between=None, order=range(TT)):
                wh, wl = wn(w_hi, s), wn(w_lo, s)
                for t in order:
                    if before is not None:
                        before(t)
                    for hf in range(2):
                        cs = slice(hf * HALF, (hf + 1) * HALF)
                        for k in range(2):
                            ts = slice(t * P, (t + 1) * P)
                            dst = bank[2 * t + hf][:, :]
                            pe.matmul(dst, lh[:, k, ts], wh[:, k, cs], start=(first and k == 0), stop=False)
                            pe.matmul(dst, lh[:, k, ts], wl[:, k, cs], start=False, stop=False)
                            mm = pe.matmul(dst, ll[:, k, ts], wh[:, k, cs], start=False, stop=(last and k == 1))
                        if last:
                            mm.then_inc(acc_done, 1)
                        if between is not None and hf == 0:
                            between(t)
                if not last:
                    mm.then_inc(block_used, 1)

            pe.sem_inc(acc_free, 8)
            pe.wait_ge(ones_set, 1)
            with pe.Fori(0, WARM_UP):
                pe.matmul(bank[7][:, 0:P], ones_dv[:, :], ones_dv[:, :], start=True, stop=True)
            pe.wait_ge(xw_ready, 1)
            wh, wl = wn(w_hi, 0), wn(w_lo, 0)
            for k in range(2):
                if k == 0:
                    pe.wait_ge(block0_low, 1)
                else:
                    arrived(0)
                for t in range(TT):
                    ts = slice(t * P, (t + 1) * P)
                    for hf in range(2):
                        cs = slice(hf * HALF, (hf + 1) * HALF)
                        dst = bank[2 * t + hf][:, :]
                        pe.matmul(dst, xw_hi[:, k, ts], wh[:, k, cs], start=(k == 0), stop=False)
                        pe.matmul(dst, xw_hi[:, k, ts], wl[:, k, cs], start=False, stop=False)
                        mm = pe.matmul(dst, xw_lo[:, k, ts], wh[:, k, cs], start=False, stop=False)
            mm.then_inc(block_used, 1)
            for b in range(1, B_QK):
                i, j = b // 4, b % 4
                arrived(b)
                if b < 4:
                    pe.wait_ge(xw_ready, j + 1)
                if b == 4:
                    pe.wait_ge(diag_ready, TT)
                    pe.wait_ge(acc_free, 8 + 1)
                    for t in range(TT):
                        mm = pe.matmul(bank[0][:, t * P:(t + 1) * P], ones_dv[:, :], rms_diag[:, t, :], start=True, stop=True)
                    mm.then_inc(row_done, 1)

                def free(t):
                    if b == 4:
                        pe.wait_ge(acc_free, 8 + 2 * t + 2)
                        if t == 0:
                            pe.wait_ge(row_ready, 1)
                ks = slice(2 * j, 2 * j + 2)
                block_N(j % 2, xw_hi[:, ks, :], xw_lo[:, ks, :], j == 0, j == 3, free,
                        order=(1, 2, 3, 0) if b == 4 else range(TT))

            pe.wait_ge(lr_w_ready, 1)
            pe.wait_ge(xt_ready, 4)
            pe.wait_ge(ident_landed, 16)
            pe.wait_ge(acc_free, 8 + 8 + 5)
            for k in range(KD):
                pe.matmul(bank[4][:, :], lr_w[:, k, :], xt_hi[:, k, :], start=(k == 0), stop=False)
                mm = pe.matmul(bank[4][:, :], lr_w[:, k, :], xt_lo[:, k, :], start=False, stop=(k == KD - 1))
            mm.then_inc(lr_done, 1)

            def queries_or_keys(i):
                for j in range(2):
                    arrived(i * 2 + (B_QK + j))
                    for t in range(2):
                        n = 2 * j + t
                        pe.wait_ge(tile_free, i * 4 + (n + 1))
                        tile_T(bank[n][:, :], wk(w_hi, j), wk(w_lo, j), t, xt_hi, xt_lo).then_inc(tile_done, 1)

            pe.wait_ge(acc_free, 8 + 16)
            pe.sem_inc(tile_free, 4)
            queries_or_keys(0)
            pe.wait_ge(gk2_ready, 1)
            pe.wait_ge(glr_ready, 1)
            for hd in range(HEADS):
                pe.matmul(bank[4 + hd][:, :], gk2[:, hd * DK:(hd + 1) * DK], glr[:, :], start=True, stop=True
                          ).then_inc(z_done, 1)
            queries_or_keys(1)

            pe.wait_ge(ones_set, 1)
            pe.wait_ge(swt_masked, 1)
            with pe.Fori(0, HEADS) as i:
                def gate_tile(j, t):
                    n = 2 * j + t
                    pe.wait_ge(tile_free, i * 4 + (8 + n + 3))
                    tile_T(bank[t][:, :], wk(w_hi, j), wk(w_lo, j), t, xt_hi, xt_lo).then_inc(tile_done, 1)

                def mix(q):
                    w = swt[:, bass.ds(i * 2 + q, 1), :].rearrange("p a t -> p (a t)")
                    for n in range(TT):
                        mm = pe.matmul(bank[4 - q][:, n * P:(n + 1) * P], vns[:, n, q * P:(q + 1) * P], w,
                                       start=True, stop=True)
                    mm.then_inc(mixed_done, 1)

                arrived(i * 2 + B_RU)
                gate_tile(0, 0)
                gate_tile(0, 1)
                arrived(i * 2 + (B_RU + 1))
                gate_tile(1, 0)
                pe.wait_ge(decayed, i * 4 + 4)
                for t in range(TT):
                    mm = pe.transpose(bank[4][:, t * P:(t + 1) * P], rest[:, 2 * t:2 * t + 2, :].rearrange("p c t -> p (c t)"),
                                      ident[:, :])
                mm.then_inc(kend_turned, 1)
                for n in range(NCH):
                    r0 = (n % 2) * CHUNK
                    mm = pe.matmul(bank[5][r0:r0 + CHUNK, n * CHUNK:(n + 1) * CHUNK], cum[:, n, :], expb[:, n, :],
                                   start=True, stop=True)
                mm.then_inc(scores_done, 1)
                gate_tile(1, 1)
                pe.wait_ge(ken_ready, i + 1)
                pe.wait_ge(staged, i * 2 + 2)
                pe.wait_ge(sct_ready, i + 1)
                for n in range(NCH - 1):
                    if n >= 4:
                        pe.wait_ge(state_ready, i * 7 + (n - 3))
                    r0 = (n % 2) * CHUNK
                    mm = pe.matmul(bank[KV_BANKS[n % 4]][:, 0:DV],
                                   ken[r0:r0 + CHUNK, n // 2, :], vst[r0:r0 + CHUNK, n // 2, :], start=True, stop=True)
                    if n % 2 == 1 or n == NCH - 2:
                        mm.then_inc(kv_done, 1)
                for q in range(2):
                    qs = slice(q * P, (q + 1) * P)
                    for t in range(TT):
                        pe.matmul(bank[6 + q][:, t * P:(t + 1) * P], vst[:, t, qs], sct[:, t, :],
                                  start=(t == 0), stop=(t == 0), skip_group_check=True)
                        for n in (2 * t, 2 * t + 1):
                            if n > 0:
                                if q == 0:
                                    pe.wait_ge(state_ready, i * 7 + n)
                                mm = pe.matmul(bank[6 + q][:, n * CHUNK:(n + 1) * CHUNK], state[:, n - 1, qs], expb[:, n, :],
                                               start=False, stop=True, skip_group_check=True)
                    mm.then_inc(o_done, 1)
                mix(0)
                mix(1)
                pe.wait_ge(osq_ready, i + 1)
                pe.matmul(bank[2][:, :], ones_dv[:, :], osq[:, :], start=True, stop=True).then_inc(ms_done, 1)

            pe.wait_ge(tile_free, 4 + 24)
            with pe.Fori(0, KD // 2) as i:
                for j in range(2):
                    arrived(i * 4 + (B_MERGE + j))
                    for t in range(2):
                        n = 2 * j + t
                        pe.wait_ge(tile_free, i * 4 + (24 + n + 1))
                        if n == 2:
                            pe.wait_ge(osd_ready, HEADS)
                        if n == 3:
                            pe.wait_ge(ya_ready, KD)
                        tile_T(bank[n][:, :], wk(w_hi, j), wk(w_lo, j), t, xt_hi, xt_lo).then_inc(tile_done, 1)
                pe.wait_ge(branch_free, i * 2 + 1)
                for j, (yh, yl) in enumerate(((ya_hi, ya_lo), (yb_hi, yb_lo))):
                    arrived(i * 4 + (B_MERGE + 2 + j))
                    for t in range(2):
                        tile_T(bank[4 + 2 * j + t][:, :], wk(w_hi, j), wk(w_lo, j), t, yh, yl).then_inc(branch_done, 1)

            pe.wait_ge(tile_free, 4 + 40)
            for j in range(4):
                arrived(B_OUT + j)
                pe.wait_ge(branch_free, 2 * j + 3)
                ks = slice(2 * j, 2 * j + 2)

                def products_read(t):
                    if j == 0 and t >= 2:
                        pe.wait_ge(prod_ready, 2 * KD - 2 + 2 * (t - 2))

                def turn_h(t):
                    if j == 3 and t >= 2:
                        turn(hn[:, t - 2, :], 2 * (t - 2), t - 2)
                block_N(j % 2, mg_hi[:, ks, :], mg_lo[:, ks, :], j == 0, j == 3, products_read, turn_h)

            s0, s1 = slice(0, SEQ // 2), slice(SEQ // 2, SEQ)
            arrived(B_FFN)
            pe.wait_ge(h0_low, 2)
            pe.wait_ge(xt_ready, 4 + 2)
            for t in range(2):
                tile_T(bank[t][:, s0], wk(w_hi, 0), wk(w_lo, 0), t, xt_hi, xt_lo, s0)
            turn(hn[:, 0, :], 4, 2)
            arrived(B_FFN + 1)
            for t in range(2):
                tile_T(bank[2 + t][:, s0], wk(w_hi, 1), wk(w_lo, 1), t, xt_hi, xt_lo, s0)
                if t == 0:
                    turn(hn[:, 1, :], 6, 3)
            pe.wait_ge(xt_ready, 4 + 6)
            for t in range(2):
                tile_T(bank[t][:, s1], wk(w_hi, 0), wk(w_lo, 0), t, xt_hi, xt_lo, s1).then_inc(gate_done, 1)
            for t in range(2):
                tile_T(bank[2 + t][:, s1], wk(w_hi, 1), wk(w_lo, 1), t, xt_hi, xt_lo, s1).then_inc(up_done, 1)
            with pe.Fori(1, FFN_IT) as i:
                arrived(i * 2 + B_FFN)
                for t in range(2):
                    pe.wait_ge(sil_ready, i * 2 + (t - 1))
                    tile_T(bank[t][:, :], wk(w_hi, 0), wk(w_lo, 0), t, xt_hi, xt_lo).then_inc(gate_done, 1)
                arrived(i * 2 + (B_FFN + 1))
                for t in range(2):
                    pe.wait_ge(act_ready, i * 2 + (t - 1))
                    tile_T(bank[2 + t][:, :], wk(w_hi, 1), wk(w_lo, 1), t, xt_hi, xt_lo).then_inc(up_done, 1)

            def down(m, s, first=False, last=False):
                arrived(m + B_DOWN)
                pe.wait_ge(al_ready, m + 1)

                def free(t):
                    if first and t == 0:
                        pe.wait_ge(sil_ready, KF)
                    if first and t == 1:
                        pe.wait_ge(act_ready, KF)
                block_N(s, ah[s], al[s], first, last, free)

            down(0, 0, first=True)
            with pe.Fori(0, 4) as i:
                down(i * 2 + 1, 1)
                down(i * 2 + 2, 0)
            down(DOWN_BLKS - 2, 1)
            down(DOWN_BLKS - 1, 0, last=True)


def _t_block(w, c0):
    return w[:, c0:c0 + 256].reshape(KD, P, 256).transpose(1, 0, 2).reshape(P, BLK)


def _n_block(w, j, c0=0):
    return w[256 * j:256 * (j + 1), c0:c0 + D].reshape(2, P, D).transpose(1, 0, 2).reshape(P, BLK)


def _tiles(v):
    return v.reshape(-1, P).T


def _four(a, axis, n=4):
    shape = list(a.shape)
    shape[axis] = P
    out = np.zeros(shape, a.dtype)
    for c in range(n):
        at = [slice(None)] * a.ndim
        at[axis] = slice(32 * c, 32 * c + LOWRANK)
        out[tuple(at)] = a
    return out


def kernel(x, norm1_w, w_in, b_in, sgu_ln_w, sgu_ln_b, sgu_w, sgu_b, w_gk2, b_gk, gla_norm_w,
           w_branch_a, w_branch_b, w_out, norm2_w, w_ffn_gate, w_ffn_up, w_ffn_down, final_norm_w):
    import concourse.bacc as bacc
    from concourse.bass_utils import run_bass_kernel_spmd

    f = np.asarray
    x2, wi, bi = f(x)[0], f(w_in)[0], f(b_in)[0]
    wa, wb, wo = f(w_branch_a)[0], f(w_branch_b)[0], f(w_out)[0]
    wg, wu, wd = f(w_ffn_gate)[0], f(w_ffn_up)[0], f(w_ffn_down)[0]

    blocks = [_n_block(wi, j, C_VG) for j in range(4)] + [_n_block(wi, j, C_V) for j in range(4)]
    blocks += [_t_block(wi, C_Q + 256 * j) for j in range(4)]
    for i in range(4):
        blocks += [_t_block(wi, C_R + 256 * i), _t_block(wi, C_U + 256 * i)]
    for i in range(4):
        blocks += [_t_block(wi, C_GA + 256 * i), _t_block(wi, C_GB + 256 * i),
                   _t_block(wa, 256 * i), _t_block(wb, 256 * i)]
    blocks += [_n_block(wo, j) for j in range(4)]
    for i in range(FFN_IT):
        blocks += [_t_block(wg, 256 * i), _t_block(wu, 256 * i)]
    blocks += [_n_block(wd, j) for j in range(DOWN_BLKS)]

    cols = np.concatenate([
        _tiles(bi[C_Q:C_Q + D]), _four(bi[C_LR:C_LR + LOWRANK, None], 0, 3), _tiles(bi[C_R:C_R + D]), _tiles(bi[C_U:C_U + D]),
        _tiles(bi[C_GA:C_GA + D]), _tiles(bi[C_GB:C_GB + D]), _tiles(f(b_gk)[0]), _tiles(f(gla_norm_w)[0]),
        _tiles(f(norm1_w)[0]), _tiles(f(norm2_w)[0])], axis=1)
    tok = np.arange(P)
    causal = ((tok[:, None] <= tok[None, :]) & (tok[:, None] // CHUNK == tok[None, :] // CHUNK)).astype(np.float32)

    arrays = {
        "x": x2,
        "x_t": x2.T.reshape(KD, P, SEQ).transpose(1, 0, 2),
        "wstream": np.stack(blocks),
        "w_lr": _four(wi[:, C_LR:C_LR + LOWRANK].reshape(KD, P, LOWRANK).transpose(1, 0, 2), 2),
        "cols": cols,
        "vbias": np.concatenate([bi[C_VG:C_VG + D], bi[C_V:C_V + D]]),
        "lnw": f(sgu_ln_w)[0], "lnb": f(sgu_ln_b)[0],
        "sgub": f(sgu_b)[0].reshape(-1),
        "sgu_wt": f(sgu_w)[0].transpose(2, 0, 1),
        "w_gk2": _four(f(w_gk2)[0], 0),
        "ident_d": np.eye(P, dtype=np.float32),
        "causal_d": causal,
        "finalw": f(final_norm_w),
    }
    nc = bacc.Bacc("TRN2", target_bir_lowering=False, num_devices=1)
    arrays = {k: np.ascontiguousarray(a) for k, a in arrays.items()}
    aps = {k: nc.dram_tensor(k, a.shape, mybir.dt.from_np(a.dtype), kind="ExternalInput").ap() for k, a in arrays.items()}
    aps["out"] = nc.dram_tensor("out", (SEQ, D), F32, kind="ExternalOutput").ap()
    build(nc, **aps)
    r = run_bass_kernel_spmd(nc, [arrays], core_ids=[0])
    return r.results[0]["out"].reshape(1, SEQ, D)
```
